# Optimizing a Trainium2 kernel written in Bass

```python
import math
import jax
import jax.numpy as jnp
from jax import lax
import numpy as np

D_MODEL = 1024
BATCH = 1
SEQ = 1024
DEPTH = 2

GRID_W = 64
CTX_LEN = 256
N_MIXERS = 4
N_A = (DEPTH + 3) // N_MIXERS
N_B = (DEPTH + 2) // N_MIXERS
N_C = (DEPTH + 1) // N_MIXERS
N_D = DEPTH // N_MIXERS
EPS = 1e-6
ROPE_THETA = 10000.0
Q_BLOCK = 128

D_RNN = 1280
RG_BLOCKS = 8
RG_BW = D_RNN // RG_BLOCKS
RG_CONV = 4
RG_CONV_LEFT = 2
RG_C = 8.0

NA_HEADS = 16
NA_DH = D_MODEL // NA_HEADS
NA_KR = 8
NA_KC = 16

GQA_HEADS = 16
GQA_KV = 4
GQA_GROUP = GQA_HEADS // GQA_KV
GQA_DH = D_MODEL // GQA_HEADS

DIFF_HEADS = 8
DIFF_DH = D_MODEL // (2 * DIFF_HEADS)

D_FF = 2816
FFN_CONV = 3

kernel_name = 'hybrid_interleaved_diffusion_trunk'

def rmsnorm(x, g):
    xf = x.astype(jnp.float32)
    y = xf * lax.rsqrt(jnp.mean(xf * xf, axis=-1, keepdims=True) + EPS)
    return (y * g).astype(x.dtype)

def modulate(z, shift, scale):
    return z * (1.0 + scale) + shift

def dwconv(x, w, b, left):
    K, L = w.shape[0], x.shape[1]
    xp = jnp.pad(x, ((0, 0), (left, K - 1 - left), (0, 0)))
    y = b + w[0] * xp[:, 0:L]
    for k in range(1, K):
        y = y + w[k] * xp[:, k:k + L]
    return y

def axial_rope(L, dh):
    t = jnp.arange(L)
    row = (t // GRID_W).astype(jnp.float32)
    col = (t % GRID_W).astype(jnp.float32)
    n = dh // 4
    inv = ROPE_THETA ** (-jnp.arange(n, dtype=jnp.float32) / n)
    ang = jnp.concatenate([row[:, None] * inv, col[:, None] * inv], axis=-1)
    return jnp.cos(ang), jnp.sin(ang)

def apply_rope(x, cos, sin):
    x1, x2 = jnp.split(x, 2, axis=-1)
    return jnp.concatenate([x1 * cos - x2 * sin, x1 * sin + x2 * cos], axis=-1).astype(x.dtype)

def softmax_attend(q, k, v, scale):
    s = jnp.einsum('bkgqd,bksd->bkgqs', q, k).astype(jnp.float32) * scale
    p = jax.nn.softmax(s, axis=-1).astype(v.dtype)
    return jnp.einsum('bkgqs,bksd->bkgqd', p, v)

def over_query_blocks(fn, q, q_axis, out_axis):
    L = q.shape[q_axis]
    nb = L // Q_BLOCK
    qb = q.reshape(q.shape[:q_axis] + (nb, Q_BLOCK) + q.shape[q_axis + 1:])
    o = lax.map(fn, jnp.moveaxis(qb, q_axis, 0))
    o = jnp.moveaxis(o, 0, out_axis)
    return o.reshape(o.shape[:out_axis] + (L,) + o.shape[out_axis + 2:])

def block_diag_linear(x, w, b):
    xb = x.reshape(x.shape[:-1] + (RG_BLOCKS, RG_BW))
    return jnp.einsum('blnj,njk->blnk', xb, w).reshape(x.shape) + b

def rglru_coeffs(xr, wa, ba, wx, bx, lam):
    xf = xr.astype(jnp.float32)
    r = jax.nn.sigmoid(block_diag_linear(xf, wa, ba))
    i = jax.nn.sigmoid(block_diag_linear(xf, wx, bx))
    log_a = -RG_C * r * jax.nn.softplus(-lam.astype(jnp.float32))
    return jnp.exp(log_a), jnp.sqrt(-jnp.expm1(2.0 * log_a)) * (i * xf)

def linear_scan(a, b, h0, reverse):
    def combine(e1, e2):
        a1, b1 = e1
        a2, b2 = e2
        return a1 * a2, a2 * b1 + b2
    a_cum, h = lax.associative_scan(combine, (a, b), reverse=reverse, axis=1)
    return h if h0 is None else h + a_cum * h0[:, None]

def rglru_mixer(zl, zc, w_in, conv_w, conv_b, wa, ba, wx, bx, lam, w_out, need_ctx):
    def branches(z):
        g, xr = jnp.split(z @ w_in, 2, axis=-1)
        return jax.nn.gelu(g), dwconv(xr, conv_w, conv_b, RG_CONV_LEFT)
    gl, xl = branches(zl)
    gc, xc = branches(zc)
    lat_states, ctx_states = [], []
    for d in range(2):
        rev = d == 1
        a_c, b_c = rglru_coeffs(xc, wa[d], ba[d], wx[d], bx[d], lam[d])
        s_c = linear_scan(a_c, b_c, None, rev)
        h0 = s_c[:, 0] if rev else s_c[:, -1]
        a_l, b_l = rglru_coeffs(xl, wa[d], ba[d], wx[d], bx[d], lam[d])
        lat_states.append(linear_scan(a_l, b_l, h0, rev))
        ctx_states.append(s_c)
    y_lat = (gl * (lat_states[0] + lat_states[1])) @ w_out
    y_ctx = (gc * (ctx_states[0] + ctx_states[1])) @ w_out if need_ctx else None
    return y_lat, y_ctx

def na_mixer(zl, zc, w_in, rpb, w_out, need_ctx):
    B, S, _ = zl.shape
    rows = S // GRID_W
    kr = min(NA_KR, rows)
    scale = NA_DH ** -0.5

    def heads(z):
        q, k, v = jnp.split(z @ w_in, 3, axis=-1)
        sh = lambda t: t.reshape(z.shape[0], z.shape[1], NA_HEADS, NA_DH).transpose(0, 2, 1, 3)
        return sh(q), sh(k), sh(v)

    ql, kl, vl = heads(zl)
    qc, kc, vc = heads(zc)
    grid = lambda t: t.reshape(B, NA_HEADS, rows, GRID_W, NA_DH)
    qg, kg, vg = grid(ql), grid(kl), grid(vl)

    cols = jnp.arange(GRID_W)
    col_start = jnp.clip(cols - NA_KC // 2, 0, GRID_W - NA_KC)
    col_in = (cols[None, :] >= col_start[:, None]) & (cols[None, :] < col_start[:, None] + NA_KC)
    col_idx = jnp.clip(cols[None, :] - cols[:, None] + NA_KC - 1, 0, 2 * NA_KC - 2)
    row_start = jnp.clip(jnp.arange(rows) - kr // 2, 0, rows - kr)

    def row_block(r):
        rs = row_start[r]
        qb = lax.dynamic_index_in_dim(qg, r, axis=2, keepdims=False)
        kb = lax.dynamic_slice_in_dim(kg, rs, kr, axis=2)
        vb = lax.dynamic_slice_in_dim(vg, rs, kr, axis=2)
        dr = rs + jnp.arange(kr) - r + NA_KR - 1
        bias = rpb[:, dr][:, :, col_idx].transpose(0, 2, 1, 3)
        s = jnp.einsum('bhqd,bhrkd->bhqrk', qb, kb).astype(jnp.float32) * scale + bias
        s = jnp.where(col_in[:, None, :], s, -jnp.inf)
        s_ctx = jnp.einsum('bhqd,bhcd->bhqc', qb, kc).astype(jnp.float32) * scale
        p = jax.nn.softmax(jnp.concatenate([s.reshape(B, NA_HEADS, GRID_W, kr * GRID_W), s_ctx], axis=-1), axis=-1).astype(vb.dtype)
        p_lat = p[..., :kr * GRID_W].reshape(B, NA_HEADS, GRID_W, kr, GRID_W)
        return jnp.einsum('bhqrk,bhrkd->bhqd', p_lat, vb) + jnp.einsum('bhqc,bhcd->bhqd', p[..., kr * GRID_W:], vc)

    o = lax.map(row_block, jnp.arange(rows))
    y_lat = o.transpose(1, 0, 3, 2, 4).reshape(B, S, D_MODEL) @ w_out
    y_ctx = None
    if need_ctx:
        oc = softmax_attend(qc[:, :, None], kc, vc, scale)[:, :, 0]
        y_ctx = oc.transpose(0, 2, 1, 3).reshape(B, zc.shape[1], D_MODEL) @ w_out
    return y_lat, y_ctx

def gqa_mixer(zl, zc, w_in, q_norm, k_norm, w_out, need_ctx):
    scale = GQA_DH ** -0.5
    cos, sin = axial_rope(zl.shape[1], GQA_DH)

    def heads(z):
        B, L, _ = z.shape
        q, k, v = jnp.split(z @ w_in, [GQA_HEADS * GQA_DH, (GQA_HEADS + GQA_KV) * GQA_DH], axis=-1)
        q = rmsnorm(q.reshape(B, L, GQA_KV, GQA_GROUP, GQA_DH), q_norm).transpose(0, 2, 3, 1, 4)
        k = rmsnorm(k.reshape(B, L, GQA_KV, GQA_DH), k_norm).transpose(0, 2, 1, 3)
        v = v.reshape(B, L, GQA_KV, GQA_DH).transpose(0, 2, 1, 3)
        return q, k, v

    def merge(o):
        return o.transpose(0, 3, 1, 2, 4).reshape(o.shape[0], o.shape[3], D_MODEL) @ w_out

    ql, kl, vl = heads(zl)
    qc, kc, vc = heads(zc)
    ql, kl = apply_rope(ql, cos, sin), apply_rope(kl, cos, sin)
    k_all = jnp.concatenate([kl, kc], axis=2)
    v_all = jnp.concatenate([vl, vc], axis=2)
    ol = over_query_blocks(lambda qb: softmax_attend(qb, k_all, v_all, scale), ql, 3, 3)
    y_ctx = merge(softmax_attend(qc, kc, vc, scale)) if need_ctx else None
    return merge(ol), y_ctx

def diff_mixer(zl, zc, w_in, lq1, lk1, lq2, lk2, subln_g, w_out, lambda_init, need_ctx):
    scale = DIFF_DH ** -0.5
    cos, sin = axial_rope(zl.shape[1], DIFF_DH)
    f32 = jnp.float32
    lam = (jnp.exp(jnp.sum(lq1.astype(f32) * lk1.astype(f32)))
           - jnp.exp(jnp.sum(lq2.astype(f32) * lk2.astype(f32))) + lambda_init)

    def heads(z):
        B, L, _ = z.shape
        q, k, v = jnp.split(z @ w_in, 3, axis=-1)
        q = q.reshape(B, L, DIFF_HEADS, 2, DIFF_DH).transpose(0, 2, 3, 1, 4)
        k = k.reshape(B, L, DIFF_HEADS, 2, DIFF_DH).transpose(0, 2, 3, 1, 4)
        v = v.reshape(B, L, DIFF_HEADS, 2 * DIFF_DH).transpose(0, 2, 1, 3)
        return q, k, v

    def attend(q, k, v):
        s = jnp.einsum('bhiqd,bhikd->bhiqk', q, k).astype(f32) * scale
        p = jax.nn.softmax(s, axis=-1)
        a = (p[:, :, 0] - lam * p[:, :, 1]).astype(v.dtype)
        return jnp.einsum('bhqk,bhkd->bhqd', a, v)

    def merge(o):
        o = rmsnorm(o, subln_g) * (1.0 - lambda_init)
        return o.transpose(0, 2, 1, 3).reshape(o.shape[0], o.shape[2], D_MODEL) @ w_out

    ql, kl, vl = heads(zl)
    qc, kc, vc = heads(zc)
    ql, kl = apply_rope(ql, cos, sin), apply_rope(kl, cos, sin)
    k_all = jnp.concatenate([kl, kc], axis=3)
    v_all = jnp.concatenate([vl, vc], axis=2)
    ol = over_query_blocks(lambda qb: attend(qb, k_all, v_all), ql, 3, 2)
    y_ctx = merge(attend(qc, kc, vc)) if need_ctx else None
    return merge(ol), y_ctx

def conv_ffn(z, w_up, conv_w, conv_b, w_down):
    u = dwconv(z @ w_up, conv_w, conv_b, FFN_CONV // 2)
    g, v = jnp.split(u, 2, axis=-1)
    return (jax.nn.silu(g) * v) @ w_down

def setup_inputs(seed: int = 0) -> dict:
    key = jax.random.key(seed)
    ks = iter(jax.random.split(key, 40))
    f32 = jnp.float32
    D = D_MODEL

    def nrm(shape, scale):
        return jax.random.normal(next(ks), shape, f32) * scale

    def gain(shape):
        return 1.0 + nrm(shape, 0.05)

    u = jax.random.uniform(next(ks), (N_A, 2, D_RNN), f32, 0.9, 0.999)
    return {
        'x': nrm((BATCH, SEQ, D), 1.0),
        'c': nrm((BATCH, D), 1.0),
        'ctx': nrm((BATCH, CTX_LEN, D), 1.0),
        'c_ctx': nrm((D,), 1.0),
        'mod_w': nrm((DEPTH, D, 6 * D), 0.5 * D ** -0.5),
        'mod_b': nrm((DEPTH, 6 * D), 0.02),
        'norm1_g': gain((DEPTH, D)),
        'norm2_g': gain((DEPTH, D)),
        'rg_w_in': nrm((N_A, D, 2 * D_RNN), D ** -0.5),
        'rg_conv_w': nrm((N_A, RG_CONV, D_RNN), RG_CONV ** -0.5),
        'rg_conv_b': nrm((N_A, D_RNN), 0.02),
        'rg_wa': nrm((N_A, 2, RG_BLOCKS, RG_BW, RG_BW), RG_BW ** -0.5),
        'rg_ba': nrm((N_A, 2, D_RNN), 0.02),
        'rg_wx': nrm((N_A, 2, RG_BLOCKS, RG_BW, RG_BW), RG_BW ** -0.5),
        'rg_bx': nrm((N_A, 2, D_RNN), 0.02),
        'rg_lam': jnp.log(u) - jnp.log1p(-u),
        'rg_w_out': nrm((N_A, D_RNN, D), D_RNN ** -0.5),
        'na_w_in': nrm((N_B, D, 3 * D), D ** -0.5),
        'na_rpb': nrm((N_B, NA_HEADS, 2 * NA_KR - 1, 2 * NA_KC - 1), 0.1),
        'na_w_out': nrm((N_B, D, D), D ** -0.5),
        'gqa_w_in': nrm((N_C, D, (GQA_HEADS + 2 * GQA_KV) * GQA_DH), D ** -0.5),
        'gqa_q_norm': gain((N_C, GQA_DH)),
        'gqa_k_norm': gain((N_C, GQA_DH)),
        'gqa_w_out': nrm((N_C, GQA_HEADS * GQA_DH, D), (GQA_HEADS * GQA_DH) ** -0.5),
        'diff_w_in': nrm((N_D, D, 3 * D), D ** -0.5),
        'diff_lq1': nrm((N_D, DIFF_DH), 0.1),
        'diff_lk1': nrm((N_D, DIFF_DH), 0.1),
        'diff_lq2': nrm((N_D, DIFF_DH), 0.1),
        'diff_lk2': nrm((N_D, DIFF_DH), 0.1),
        'diff_subln_g': gain((N_D, 2 * DIFF_DH)),
        'diff_w_out': nrm((N_D, D, D), D ** -0.5),
        'ffn_w_up': nrm((DEPTH, D, 2 * D_FF), D ** -0.5),
        'ffn_conv_w': nrm((DEPTH, FFN_CONV, 2 * D_FF), FFN_CONV ** -0.5),
        'ffn_conv_b': nrm((DEPTH, 2 * D_FF), 0.02),
        'ffn_w_down': nrm((DEPTH, D_FF, D), D_FF ** -0.5),
        'final_g': gain((D,)),
    }

def reference(x, c, ctx, c_ctx, mod_w, mod_b, norm1_g, norm2_g,
              rg_w_in, rg_conv_w, rg_conv_b, rg_wa, rg_ba, rg_wx, rg_bx, rg_lam, rg_w_out,
              na_w_in, na_rpb, na_w_out,
              gqa_w_in, gqa_q_norm, gqa_k_norm, gqa_w_out,
              diff_w_in, diff_lq1, diff_lk1, diff_lq2, diff_lk2, diff_subln_g, diff_w_out,
              ffn_w_up, ffn_conv_w, ffn_conv_b, ffn_w_down, final_g):
    xl, xc = x, ctx
    silu_c, silu_cc = jax.nn.silu(c), jax.nn.silu(c_ctx)
    for l in range(DEPTH):
        m, j = l % N_MIXERS, l // N_MIXERS
        need_ctx = l < DEPTH - 1
        mods = jnp.split((silu_c @ mod_w[l] + mod_b[l])[:, None, :], 6, axis=-1)
        cmods = jnp.split((silu_cc @ mod_w[l] + mod_b[l])[None, None, :], 6, axis=-1)
        zl = modulate(rmsnorm(xl, norm1_g[l]), mods[0], mods[1])
        zc = modulate(rmsnorm(xc, norm1_g[l]), cmods[0], cmods[1])
        if m == 0:
            yl, yc = rglru_mixer(zl, zc, rg_w_in[j], rg_conv_w[j], rg_conv_b[j], rg_wa[j], rg_ba[j],
                                 rg_wx[j], rg_bx[j], rg_lam[j], rg_w_out[j], need_ctx)
        elif m == 1:
            yl, yc = na_mixer(zl, zc, na_w_in[j], na_rpb[j], na_w_out[j], need_ctx)
        elif m == 2:
            yl, yc = gqa_mixer(zl, zc, gqa_w_in[j], gqa_q_norm[j], gqa_k_norm[j], gqa_w_out[j], need_ctx)
        else:
            lambda_init = 0.8 - 0.6 * math.exp(-0.3 * l)
            yl, yc = diff_mixer(zl, zc, diff_w_in[j], diff_lq1[j], diff_lk1[j], diff_lq2[j], diff_lk2[j],
                                diff_subln_g[j], diff_w_out[j], lambda_init, need_ctx)
        xl = xl + mods[2] * yl
        zl = modulate(rmsnorm(xl, norm2_g[l]), mods[3], mods[4])
        xl = xl + mods[5] * conv_ffn(zl, ffn_w_up[l], ffn_conv_w[l], ffn_conv_b[l], ffn_w_down[l])
        if need_ctx:
            xc = xc + cmods[2] * yc
            zc = modulate(rmsnorm(xc, norm2_g[l]), cmods[3], cmods[4])
            xc = xc + cmods[5] * conv_ffn(zc, ffn_w_up[l], ffn_conv_w[l], ffn_conv_b[l], ffn_w_down[l])
    return rmsnorm(xl, final_g)


_drawn_inputs = setup_inputs


def setup_inputs(seed=0):
    import zlib

    import numpy as np

    out = dict(_drawn_inputs(seed))
    spreads = {}
    factors = {'norm2_g': 2.751,
     'rg_conv_b': 2.989,
     'rg_ba': 31.759,
     'rg_bx': 8.0,
     'na_rpb': 41.196,
     'ffn_conv_b': 7.325}
    for name, (base, spread) in spreads.items():
        noise = np.random.default_rng([zlib.crc32(name.encode()), seed]).standard_normal(out[name].shape)
        drawn = base * np.exp(spread * noise) if base else spread * noise
        out[name] = jnp.asarray(drawn.astype(out[name].dtype))
    for name, factor in factors.items():
        out[name] = (out[name] * factor).astype(out[name].dtype)
    return out
```

```python
from contextlib import ExitStack

import concourse.bass as bass
from concourse import mybir

F32 = mybir.dt.float32
F32R = mybir.dt.float32r
ALU = mybir.AluOpType
ACT = mybir.ActivationFunctionType
AX_X = mybir.AxisListType.X
ds = bass.ds

P = 128
D = 1024
SEQ = 1024
CTX = 256
TOK = SEQ + CTX
KD = D // P
D_RNN = 1280
KR = D_RNN // P
RG_BW = 160
HALF = KR // 2
D_FF = 2816
KF = D_FF // P
N_MOD = 6 * KD
HEADS = 16
DH = 64
ROWS = SEQ // 64
GW = 64
NA_KR, NA_KC = 8, 16
WIN = NA_KR * GW
KEYS = WIN + CTX
EPS = 1e-6
MASKED = -1.0e30
BANK = 512
SLOT = 3 * BANK
MISC = 2 * SLOT

LAT = (0, SEQ)
CTXS = (SEQ, TOK)
STOP = 99


def chunks(ntok):
    return [(c, min(BANK, ntok - c)) for c in range(0, ntok, BANK)]


def segs(ntok):
    return [LAT] if ntok == SEQ else [LAT, CTXS]


def gate_pairs():
    out = []
    for mt in range(HALF):
        b0, b1 = mt * P // RG_BW, (mt * P + P - 1) // RG_BW
        k0, k1 = b0 * RG_BW // P, (b1 * RG_BW + RG_BW - 1) // P
        out += [(mt, kt) for kt in range(k0, k1 + 1)]
    return out


PAIRS = gate_pairs()


def gate_rects():
    out = []
    for p, (mt, kt) in enumerate(PAIRS):
        for b in range(4):
            r0, r1 = max(kt * P, b * RG_BW), min(kt * P + P, (b + 1) * RG_BW)
            c0, c1 = max(mt * P, b * RG_BW), min(mt * P + P, (b + 1) * RG_BW)
            if r0 < r1 and c0 < c1:
                out.append((p, b, r0 - kt * P, r0 - b * RG_BW, r1 - r0, c0 - mt * P, c0 - b * RG_BW, c1 - c0))
    return out


RECTS = gate_rects()

VECS = [("mod_b", 2 * N_MOD), ("norm1_g", 2 * KD), ("norm2_g", 2 * KD), ("final_g", KD), ("c", KD), ("c_ctx", KD),
        ("rg_conv_w", 4 * KR), ("rg_conv_b", KR), ("rg_ba", 2 * KR), ("rg_bx", 2 * KR), ("rg_lam", 2 * KR),
        ("ffn_conv_w", 2 * 3 * 2 * KF), ("ffn_conv_b", 2 * 2 * KF)]
VEC_AT = {}
N_VEC = 0
for _name, _rows in VECS:
    VEC_AT[_name] = N_VEC
    N_VEC += _rows
VT = (N_VEC + P - 1) // P


def prime(eng, *sems):
    for s, n in sems:
        eng.nop().then_inc(s, n)


def primed(value, start=1):
    return value + start


class Bag:
    pass


class Order:

    def __init__(self, eng, sem, base=0):
        self.eng, self.sem, self.base, self.n = eng, sem, base, 0

    def __call__(self, ins):
        self.n += 1
        ins.then_inc(self.sem, 1)
        self.eng.wait_ge(self.sem, self.base + self.n)


class Plan:

    def __init__(self, nc, at):
        self.nc, self.at = nc, at

    def put(self, name, shape, dt=F32):
        n = 4
        for s in shape[1:]:
            n *= s
        t = self.nc.alloc_sbuf_tensor_at(name, shape, dt, offset=self.at)
        self.at += (n + 31) // 32 * 32
        return t

    def same_place(self):
        return Plan(self.nc, self.at)


def build(nc, t, out):
    es = ExitStack()
    m = Bag()
    m.t = t
    m.out = out

    phase_sems = []

    def sem(name):
        phase_sems.append(nc.alloc_semaphore(name))
        return phase_sems[-1]

    def run(phase, *args):
        phase(nc, m, *args)
        nc.clear_and_free_semaphores(list(phase_sems))
        phase_sems.clear()
        nc.all_engine_barrier()

    m.sem = sem
    m.xT = nc.dram_tensor("scratch_xT", [KD, P, TOK], F32).ap()
    m.yT = nc.dram_tensor("scratch_yT", [KR, P, TOK], F32).ap()
    m.rpbT = nc.dram_tensor("scratch_rpb", [HEADS, 15, 127], F32).ap()
    m.biasT = nc.dram_tensor("scratch_bias", [HEADS, GW, 15, GW], F32).ap()

    pl = Plan(nc, (nc.sbuf_base + 63) // 64 * 64)
    m.vec = pl.put("vec", [P, VT * P])
    m.ident = pl.put("ident", [P, P])
    m.ones = pl.put("ones", [P, P])
    m.eps = pl.put("eps", [P, 1])
    m.mod = pl.put("mod", [P, 2, 2, N_MOD])
    m.ccol = pl.put("ccol", [P, KD, 2])
    m.gain = pl.put("gain", [P, 2, 2, 2, KD])
    m.gate = pl.put("gate", [P, 2, KD])
    m.mask = pl.put("mask", [P, GW])
    m.lru = pl.put("lru", [P, 6, 2 * KR])
    modring_at = pl.at
    m.modw = pl.put("modw", [P, 2, KD, P])
    bp = Plan(nc, modring_at)
    m.bias = bp.put("bias", [P, 15, GW])
    ring_at = pl.at
    m.wraw = pl.put("wraw", [P, 3, D])
    m.wH = pl.put("wH", [P, 3, D], F32R)
    m.wL = pl.put("wL", [P, 3, D], F32R)
    op = Plan(nc, ring_at)
    m.oraw = op.put("oraw", [P, 2, KR, P])
    op.at = ring_at + 3 * D * 4
    m.oH = op.put("oH", [P, 2, KR, P], F32R)
    m.oL = op.put("oL", [P, 2, KR, P], F32R)
    z_at = pl.at
    m.zH = pl.put("zH", [P, KD, TOK], F32R)
    m.zL = pl.put("zL", [P, KD, TOK], F32R)
    zp = Plan(nc, z_at)
    m.xraw = zp.put("xraw", [P, TOK // P, D])
    m.vraw = zp.put("vraw", [P, VT, P])
    m.rpb = zp.put("rpb", [P, 2, 127])
    zp = Plan(nc, z_at)
    m.outT = zp.put("outT", [P, 2, D])
    arena = pl.at

    a = Plan(nc, arena)
    m.res = a.put("res", [P, KD, TOK])
    w = a.same_place()
    m.sq = w.put("sq", [P, 2, TOK])
    m.rstd = w.put("rstd", [P, TOK])
    m.ztmp = w.put("ztmp", [P, 2, TOK])
    w = a.same_place()
    m.yraw = w.put("yraw", [P, 2, TOK])
    m.yH = w.put("yH", [P, KR - KD, TOK], F32R)
    m.yL = w.put("yL", [P, KR - KD, TOK], F32R)
    w = a.same_place()
    m.G = w.put("G", [P, TOK])
    m.V = w.put("V", [P, TOK])
    m.hH = w.put("hH", [P, 2, TOK], F32R)
    m.hL = w.put("hL", [P, 2, TOK], F32R)
    w = a.same_place()
    m.qbd = w.put("qbd", [P, ROWS, P])
    m.kT = w.put("kT", [P, TOK])
    m.v0 = w.put("v0", [P, TOK // P, P])
    m.v1 = w.put("v1", [P, SEQ // P - 1, P])
    vt_at = w.at
    m.S = w.put("S", [P, 2, KEYS])
    m.vT = Plan(nc, vt_at).put("vT", [P, TOK])
    m.pT = w.put("pT", [P, 2, KEYS])
    m.oT = w.put("oT", [P, SEQ])
    w = Plan(nc, arena)
    m.gW = w.put("gW", [P, 4, len(PAIRS), P])
    m.x = w.put("xconv", [P, HALF, TOK])
    m.TR = w.put("TR", [P, 2, TOK])
    m.TI = w.put("TI", [P, TOK])
    m.A = w.put("A", [P, TOK])
    m.GG = w.put("GG", [P, TOK])
    sm = Plan(nc, nc.sbuf_usable_end // 32 * 32 - 64)
    m.rowstat = sm.put("rowstat", [P, 2, 4])

    m.ps = es.enter_context(nc.psum_tensor("ps", [P, 8 * BANK], F32))

    with es:
        run(setup)
        run(norm, 0, 0, TOK)
        if STOP >= 2:
            run(rglru)
        if STOP >= 3:
            run(project, 0, m.t["rg_w_out"][0], KR, TOK)
            run(norm, 0, 1, TOK)
        if STOP >= 4:
            run(ffn, 0, TOK)
            run(norm, 1, 0, TOK)
        if STOP >= 5:
            run(attention)
            run(project, 1, m.t["na_w_out"][0], KD, SEQ)
            run(norm, 1, 1, SEQ)
            run(ffn, 1, SEQ)
        final(nc, m)


def vcol(m, name, i, n=1):
    at = VEC_AT[name] + i
    return m.vec[:, at:at + n]


def setup(nc, m):
    t, sem, ps = m.t, m.sem, m.ps
    x_in = [sem(f"su_x_in{i}") for i in range(TOK // P)]
    vec_in = sem("su_vec_in")
    rpb_zero, rpb_in, rpb_out = sem("su_rpb_zero"), sem("su_rpb_in"), sem("su_rpb_out")
    mod_in = [sem("su_mod_in0"), sem("su_mod_in1")]
    mod_used, mod_done = sem("su_mod_used"), sem("su_mod_done")
    const, vec_T, vec_ready, c_ready = sem("su_const"), sem("su_vec_T"), sem("su_vec_ready"), sem("su_c_ready")
    xT_done, res_ready, spilled = sem("su_xT_done"), sem("su_res_ready"), sem("su_spilled")
    v_order, a_order, lru_ready = sem("su_v_order"), sem("su_a_order"), sem("su_lru")
    act_ln = sem("su_act_ln")
    NT = TOK // P
    src = {"mod_b": t["mod_b"].rearrange("l (n p) -> (l n) p", p=P), "norm1_g": t["norm1_g"].rearrange("l (n p) -> (l n) p", p=P),
           "norm2_g": t["norm2_g"].rearrange("l (n p) -> (l n) p", p=P), "final_g": t["final_g"].rearrange("(n p) -> n p", p=P),
           "c": t["c"].rearrange("b (n p) -> (b n) p", p=P), "c_ctx": t["c_ctx"].rearrange("(n p) -> n p", p=P),
           "rg_conv_w": t["rg_conv_w"][0].rearrange("k (n p) -> (k n) p", p=P), "rg_conv_b": t["rg_conv_b"].rearrange("a (n p) -> (a n) p", p=P),
           "rg_ba": t["rg_ba"][0].rearrange("k (n p) -> (k n) p", p=P), "rg_bx": t["rg_bx"][0].rearrange("k (n p) -> (k n) p", p=P),
           "rg_lam": t["rg_lam"][0].rearrange("k (n p) -> (k n) p", p=P),
           "ffn_conv_w": t["ffn_conv_w"].rearrange("l k (n p) -> (l k n) p", p=P), "ffn_conv_b": t["ffn_conv_b"].rearrange("l (n p) -> (l n) p", p=P)}
    vec_dmas = []
    for name, rows in VECS:
        done = 0
        while done < rows:
            at = VEC_AT[name] + done
            k = min(rows - done, P - at % P)
            vec_dmas.append((at // P, at % P, k, src[name][done:done + k, :]))
            done += k

    with nc.Block() as block:
        @block.sync
        def _(sp):
            for tile, row, k, s in vec_dmas:
                sp.dma_start(m.vraw[row:row + k, tile, :], s).then_inc(vec_in, 16)
            for i in range(NT):
                s = t["x"][0, i * P:(i + 1) * P, :] if i < SEQ // P else t["ctx"][0, i * P - SEQ:(i + 1) * P - SEQ, :]
                sp.dma_start(m.xraw[:, i, :], s).then_inc(x_in[i], 16)
            for f in range(KD):
                sp.wait_ge(res_ready, f + 1)
                sp.dma_start(m.xT[f], m.res[:, f, :]).then_inc(spilled, 16)
            sp.wait_ge(spilled, 16 * KD)

        @block.gpsimd
        def _(gp):
            mo = Order(gp, const)
            mo(nc.gpsimd.memset(m.ident[:, :], 0.0))
            mo(nc.gpsimd.affine_select(out=m.ident[:, :], in_=m.ident[:, :], compare_op=ALU.not_equal, fill=1.0, base=0,
                                       pattern=[[-1, P]], channel_multiplier=1))
            mo(nc.gpsimd.memset(m.ones[:, :], 1.0))
            mo(nc.gpsimd.memset(m.eps[:, :], EPS))
            mo(nc.gpsimd.memset(m.mask[:, :], 0.0))
            for h in range(2):
                pr = m.mask[h * 64:h * 64 + 64, :]
                lo = pr[:, 0:GW - NA_KC]
                mo(nc.gpsimd.affine_select(out=lo, in_=lo, compare_op=ALU.is_ge, fill=MASKED, base=NA_KC // 2,
                                           pattern=[[1, GW - NA_KC]], channel_multiplier=-1))
                hi = pr[:, NA_KC:GW]
                mo(nc.gpsimd.affine_select(out=hi, in_=hi, compare_op=ALU.is_gt, fill=MASKED, base=NA_KC // 2 - NA_KC,
                                           pattern=[[-1, GW - NA_KC]], channel_multiplier=1))
            nc.gpsimd.memset(m.rpb[:, :, :], 0.0).then_inc(rpb_zero, 1)
            gp.wait_ge(rpb_zero, 1)
            half = HEADS * 15 // 2
            gp.dma_start(m.rpb[0:half, :, 48:79], t["na_rpb"][0].rearrange("h r c -> (h r) c").rearrange("(p a) c -> p a c", a=2)).then_inc(rpb_in, 16)
            gp.wait_ge(rpb_in, 16)
            gp.dma_start(m.rpbT.rearrange("h r c -> (h r) c").rearrange("(p a) c -> p a c", a=2), m.rpb[0:half, :, :]).then_inc(rpb_out, 16)
            for q in range(2 * KD):
                if q >= 2:
                    gp.wait_ge(mod_used, q - 1)
                gp.dma_start(m.modw[:, q % 2, :, :], t["mod_w"][0].rearrange("(k p) n -> p k n", p=P)[:, :, q * P:(q + 1) * P]).then_inc(mod_in[q % 2], 16)
            gp.wait_ge(rpb_out, 16)

        @block.tensor
        def _(pe):
            pe.wait_ge(const, 2)
            pe.wait_ge(vec_in, 16 * len(vec_dmas))
            for i in range(VT):
                n = min(P, N_VEC - i * P)
                ins = nc.tensor.transpose(ps[:, MISC + i * P:MISC + i * P + n], m.vraw[0:n, i, :], m.ident[0:n, 0:n])
            ins.then_inc(vec_T, 1)
            for f in range(KD):
                s = f % 2
                if f >= 2:
                    pe.wait_ge(res_ready, f - 1)
                for i in range(NT):
                    if f == 0:
                        pe.wait_ge(x_in[i], 16)
                    ins = nc.tensor.transpose(ps[:, s * SLOT + i * P:s * SLOT + i * P + P], m.xraw[:, i, f * P:(f + 1) * P], m.ident[:, :])
                ins.then_inc(xT_done, 1)
            pe.wait_ge(c_ready, 2)
            pe.wait_ge(vec_ready, 2)
            for q in range(2 * KD):
                pe.wait_ge(mod_in[q % 2], 16 * (q // 2 + 1))
                for k in range(KD):
                    ins = nc.tensor.matmul(ps[:, MISC + BANK + 2 * q:MISC + BANK + 2 * q + 2], m.modw[:, q % 2, k, :], m.ccol[:, k, :],
                                           start=(k == 0), stop=(k == KD - 1))
                ins.then_inc(mod_used, 1)

        @block.scalar
        def _(act):
            act.wait_ge(vec_T, 1)
            nc.scalar.activation(m.vec[:, 0:BANK], ps[:, MISC:MISC + BANK], ACT.Copy).then_inc(vec_ready, 1)
            nc.scalar.activation(m.vec[:, BANK:N_VEC], ps[:, MISC + BANK:MISC + N_VEC], ACT.Copy).then_inc(vec_ready, 1)
            act.wait_ge(vec_ready, 2)
            for s, name in enumerate(("c", "c_ctx")):
                nc.scalar.activation(m.ccol[:, :, s], vcol(m, name, 0, KD), ACT.Silu).then_inc(c_ready, 1)
            lam = vcol(m, "rg_lam", 0, 2 * KR)
            ao = Order(act, a_order)
            ao(nc.scalar.activation(m.lru[:, 0, :], lam, ACT.Abs))
            ao(nc.scalar.activation(m.lru[:, 0, :], m.lru[:, 0, :], ACT.Exp, scale=-1.0))
            act.wait_ge(lru_ready, 1)
            nc.scalar.activation(m.lru[:, 2, :], m.lru[:, 1, :], ACT.Ln).then_inc(act_ln, 1)
            act.wait_ge(act_ln, 1)
            nc.scalar.activation(m.lru[:, 3, :], m.lru[:, 2, :], ACT.Tanh, scale=0.5).then_inc(act_ln, 1)

        @block.vector
        def _(dve):
            vo = Order(dve, v_order)
            for f in range(KD):
                dve.wait_ge(xT_done, f + 1)
                nc.vector.tensor_copy(m.res[:, f, :], ps[:, (f % 2) * SLOT:(f % 2) * SLOT + TOK]).then_inc(res_ready, 1)
            lru_constants(nc, m, dve, vo, a_order, lru_ready, act_ln)
            dve.wait_ge(mod_used, 2 * KD)
            for s in range(2):
                vo(nc.vector.tensor_tensor(m.mod[:, 0, s, 0:2 * KD], ps[:, MISC + BANK + s:MISC + BANK + 4 * KD:2],
                                           vcol(m, "mod_b", 0, 2 * KD), ALU.add))
            for s in range(2):
                vo(nc.vector.scalar_tensor_tensor(out=m.gain[:, 0, 0, s, :], in0=m.mod[:, 0, s, KD:2 * KD], scalar=1.0,
                                                  in1=vcol(m, "norm1_g", 0, KD), op0=ALU.add, op1=ALU.mult))


def lru_constants(nc, m, dve, vo, a_order, lru_ready, act_ln):
    lam = vcol(m, "rg_lam", 0, 2 * KR)
    r = [m.lru[:, i, :] for i in range(6)]
    dve.wait_ge(a_order, 2)
    nc.vector.tensor_scalar(r[1], r[0], 1.0, None, ALU.add).then_inc(lru_ready, 1)
    dve.wait_ge(lru_ready, 1)
    dve.wait_ge(act_ln, 2)
    vo(nc.vector.tensor_scalar(r[4], r[3], -1.0, 1.0, ALU.mult, ALU.add))
    vo(nc.vector.reciprocal(r[4], r[4]))
    vo(nc.vector.scalar_tensor_tensor(out=r[3], in0=r[3], scalar=2.0, in1=r[4], op0=ALU.mult, op1=ALU.mult))
    vo(nc.vector.tensor_tensor(r[3], r[3], r[0], ALU.subtract))
    vo(nc.vector.reciprocal(r[1], r[1]))
    vo(nc.vector.tensor_tensor(r[3], r[3], r[1], ALU.mult))
    vo(nc.vector.tensor_tensor(r[2], r[2], r[3], ALU.subtract))
    vo(nc.vector.tensor_scalar(r[1], lam, -1.0, 0.0, ALU.mult, ALU.max))
    vo(nc.vector.tensor_tensor(r[5], r[1], r[2], ALU.add))
    vo(nc.vector.tensor_scalar(r[0], r[5], 2.0, None, ALU.mult))
    vo(nc.vector.tensor_scalar(r[1], r[5], 4.0, None, ALU.mult))
    vo(nc.vector.tensor_scalar(r[2], r[5], -4.0, None, ALU.mult))
    vo(nc.vector.tensor_scalar(r[3], vcol(m, "rg_ba", 0, 2 * KR), 0.5, None, ALU.mult))
    vo(nc.vector.tensor_scalar(r[4], vcol(m, "rg_bx", 0, 2 * KR), 0.5, None, ALU.mult))


def norm_stats(nc, m, tag, ntok):
    s = Bag()
    s.sq_ready, s.sq_used, s.sum_done, s.root, s.rstd = [m.sem(f"{tag}_{n}") for n in ("sq_ready", "sq_used", "sum_done", "root", "rstd")]

    def act_part(act):
        for k in range(KD):
            if k >= 2:
                act.wait_ge(s.sq_used, k - 1)
            nc.scalar.activation(m.sq[:, k % 2, 0:ntok], m.res[:, k, 0:ntok], ACT.Square).then_inc(s.sq_ready, 1)
        act.wait_ge(s.sum_done, 1)
        nc.scalar.activation(m.rstd[:, 0:ntok], m.ps[:, 0:ntok], ACT.Sqrt, bias=m.eps[:, :], scale=1.0 / D).then_inc(s.root, 1)

    def pe_part(pe):
        for k in range(KD):
            pe.wait_ge(s.sq_ready, k + 1)
            for c, n in chunks(ntok):
                ins = nc.tensor.matmul(m.ps[:, c:c + n], m.ones[:, :], m.sq[:, k % 2, c:c + n], start=(k == 0), stop=(k == KD - 1))
            ins.then_inc(s.sq_used, 1)
            if k == KD - 1:
                pe.wait_ge(s.sq_used, KD)
                pe.nop().then_inc(s.sum_done, 1)

    def dve_part(dve):
        dve.wait_ge(s.root, 1)
        nc.vector.reciprocal(m.rstd[:, 0:ntok], m.rstd[:, 0:ntok]).then_inc(s.rstd, 1)
        dve.wait_ge(s.rstd, 1)

    s.act, s.pe, s.dve = act_part, pe_part, dve_part
    return s


def norm(nc, m, l, which, ntok):
    tag = f"n{l}{which}"
    st = norm_stats(nc, m, tag, ntok)
    scaled, high, low = m.sem(tag + "_scaled"), m.sem(tag + "_high"), m.sem(tag + "_low")
    shift = 3 * which * KD

    with nc.Block() as block:
        @block.scalar
        def _(act):
            st.act(act)
            for k in range(KD):
                act.wait_ge(scaled, k + 1)
                for s, (a, b) in enumerate(segs(ntok)):
                    ins = nc.scalar.activation(m.zH[:, k, a:b], m.ztmp[:, k % 2, a:b], ACT.Identity,
                                               bias=m.mod[:, l, s, shift + k:shift + k + 1])
                    ins.then_inc(high, 1)

        @block.tensor
        def _(pe):
            st.pe(pe)

        @block.vector
        def _(dve):
            st.dve(dve)
            ns = len(segs(ntok))
            for k in range(KD + 1):
                if k < KD:
                    if k >= 2:
                        dve.wait_ge(low, ns * (k - 1))
                    for s, (a, b) in enumerate(segs(ntok)):
                        ins = nc.vector.scalar_tensor_tensor(out=m.ztmp[:, k % 2, a:b], in0=m.res[:, k, a:b],
                                                             scalar=m.gain[:, l, which, s, k:k + 1], in1=m.rstd[:, a:b],
                                                             op0=ALU.mult, op1=ALU.mult)
                        if s == ns - 1:
                            ins.then_inc(scaled, 1)
                if k > 0:
                    j = k - 1
                    dve.wait_ge(high, ns * (j + 1))
                    for s, (a, b) in enumerate(segs(ntok)):
                        nc.vector.scalar_tensor_tensor(out=m.zL[:, j, a:b], in0=m.ztmp[:, j % 2, a:b],
                                                       scalar=m.mod[:, l, s, shift + j:shift + j + 1],
                                                       in1=m.zH[:, j, a:b].bitcast(F32), op0=ALU.add, op1=ALU.subtract).then_inc(low, 1)


def product(nc, ps, slot, ntok, wH, wL, rH, rL, K):
    last = None
    for k in range(K):
        for i, (w, r) in enumerate(((wH, rH), (wH, rL), (wL, rH))):
            for c, n in chunks(ntok):
                last = nc.tensor.matmul(ps[:, slot * SLOT + c:slot * SLOT + c + n], w(k), r(k)[:, c:c + n],
                                        start=(k == 0 and i == 0), stop=(k == K - 1 and i == 2))
    return last


def taps(nc, dve, order, dst, src, ws, ntok):
    for shift, w in ws:
        for a, b in segs(ntok):
            lo, hi = max(a, a - shift), min(b, b - shift)
            order(nc.vector.scalar_tensor_tensor(out=dst[:, lo:hi], in0=src[:, lo + shift:hi + shift], scalar=w, in1=dst[:, lo:hi],
                                                 op0=ALU.mult, op1=ALU.add))


def rglru(nc, m):
    t, sem, ps = m.t, m.sem, m.ps
    raw_in = [sem(f"rg_raw_in{i}") for i in range(3)]
    w_high, w_ready, w_used = sem("rg_w_high"), sem("rg_w_ready"), sem("rg_w_used")
    unit_done, psum_free = sem("rg_unit_done"), [sem("rg_psum_free0"), sem("rg_psum_free1")]
    gw_zero, gw_in = sem("rg_gw_zero"), sem("rg_gw_in")
    x_mid, x_ready, taps_order = sem("rg_x_mid"), sem("rg_x_ready"), sem("rg_taps_order")
    g_ready, tr_ready, ti_ready, a_ready, t2_ready, sq_ready = [sem("rg_" + n) for n in ("g_ready", "tr_ready", "ti_ready", "a_ready", "t2_ready", "sq_ready")]
    scans, dir_order, y_ready, y_out = sem("rg_scans"), sem("rg_dir_order"), sem("rg_y_ready"), sem("rg_y_out")
    mod_in, mod_used, mod_copied = [sem("rg_mod_in0"), sem("rg_mod_in1")], sem("rg_mod_used"), sem("rg_mod_copied")
    bias_made, y_stored = sem("rg_bias_made"), sem("rg_y_stored")

    seq = [("x", 0)]
    for j in range(HALF):
        if j + 1 < HALF:
            seq.append(("x", j + 1))
        seq.append(("g", j))
        seq += [("r0", j), ("i0", j), ("r1", j), ("i1", j)]
    U = len(seq)
    assert U % 2 == 0
    blocks = [(k, j) for k, j in seq if k in "xg"]
    NB = len(blocks)
    per_slot = [len(range(s, NB, 3)) for s in range(3)]
    mods = [3, 3, 3, 3, 4]
    MH = sum(mods)
    GR = len(RECTS) * 4
    w_in = t["rg_w_in"][0].rearrange("(k p) n -> p k n", p=P)
    mod_w = t["mod_w"][0].rearrange("(k p) n -> p k n", p=P)
    gate_w = {"r": t["rg_wa"][0], "i": t["rg_wx"][0]}
    kinds = ["r0", "i0", "r1", "i1"]
    n_taps = 6

    with nc.Block() as block:
        @block.sync
        def _(sp):
            with sp.Fori(0, 2) as h:
                h4 = sp.snap(4 * h)
                for b, (kind, j) in enumerate(blocks):
                    if b == 3:
                        sp.wait_ge(gw_zero, 1)
                        sp.wait_ge(unit_done, primed(U * h))
                        for p, blk, r, rb, nr, c, cb, ncol in RECTS:
                            for g, gk in enumerate(kinds):
                                srcw = gate_w[gk[0]][int(gk[1])]
                                sp.dma_start(m.gW[r:r + nr, g, p, c:c + ncol], srcw[ds(h4 + blk, 1), rb:rb + nr, cb:cb + ncol].rearrange("a r c -> (a r) c")).then_inc(gw_in, 16)
                    if b == 0 or b >= 3:
                        sp.wait_ge(w_ready, primed(NB * h + b - 2 if b >= 3 else NB * h))
                    col = (0 if kind == "g" else D_RNN) + P * j
                    sp.dma_start(m.wraw[:, b % 3, :].rearrange("p (k n) -> p k n", k=KD), w_in[:, :, ds(HALF * P * h + col, P)]).then_inc(raw_in[b % 3], 16)

        @block.gpsimd
        def _(gp):
            prime(gp, (y_stored, 1))
            nc.gpsimd.memset(m.gW[:, :, :, :], 0.0).then_inc(gw_zero, 1)
            with gp.Fori(0, GW) as q:
                gp.dma_start(m.biasT[:, ds(q, 1), :, :].rearrange("h a r c -> h (a r) c"), m.rpbT[:, :, ds(GW - 1 - q, GW)]).then_inc(bias_made, 16)
            with gp.Fori(0, 2) as h:
                q = 0
                for j in range(HALF):
                    for _ in range(mods[j]):
                        gp.wait_ge(mod_used, primed(MH * h + q - 1 if q >= 2 else MH * h))
                        gp.dma_start(m.modw[:, q % 2, :, :], mod_w[:, :, ds(MH * P * h + (2 * KD + q) * P, P)]).then_inc(mod_in[q % 2], 16)
                        q += 1
                    gp.wait_ge(y_ready, primed(HALF * h + j + 1))
                    gp.dma_start(m.yT[ds(HALF * h + j, 1)].rearrange("a p t -> (a p) t"), m.TR[:, 0, :]).then_inc(y_out, 16)
                    gp.wait_ge(y_out, 16 * HALF * h + 16 * (j + 1))
                    gp.nop().then_inc(y_stored, 1)
            gp.wait_ge(bias_made, 16 * GW)

        @block.tensor
        def _(pe):
            prime(pe, (w_used, 1), (unit_done, 1), (mod_used, 1))
            with pe.Fori(0, 2) as h:
                b = q = 0
                for u, (kind, j) in enumerate(seq):
                    s = u % 2
                    pe.wait_ge(psum_free[s], primed((U // 2) * h + u // 2))
                    if kind in "xg":
                        pe.wait_ge(w_ready, primed(NB * h + b + 1))
                        wH = m.wH[:, b % 3, :]
                        wL = m.wL[:, b % 3, :]
                        ins = product(nc, ps, s, TOK, lambda k: wH[:, k * P:(k + 1) * P], lambda k: wL[:, k * P:(k + 1) * P],
                                      lambda k: m.zH[:, k, :], lambda k: m.zL[:, k, :], KD)
                        ins.then_inc(unit_done, 1)
                        pe.wait_ge(unit_done, primed(U * h + u + 1))
                        pe.nop().then_inc(w_used, 1)
                        b += 1
                    else:
                        pe.wait_ge(x_ready, HALF * h + min(j + 2, HALF))
                        if j == 0 and kind == "r0":
                            pe.wait_ge(gw_in, 16 * GR * h + 16 * GR)
                        steps = [(p, kt) for p, (mt, kt) in enumerate(PAIRS) if mt == j]
                        for n, (p, kt) in enumerate(steps):
                            for c, w in chunks(TOK):
                                ins = nc.tensor.matmul(ps[:, s * SLOT + c:s * SLOT + c + w], m.gW[:, kinds.index(kind), p, :],
                                                       m.x[:, kt, c:c + w], start=(n == 0), stop=(n == len(steps) - 1))
                        ins.then_inc(unit_done, 1)
                        if kind == "i1":
                            for _ in range(mods[j]):
                                pe.wait_ge(mod_in[q % 2], (16 * MH // 2) * h + 16 * (q // 2 + 1))
                                if q == 0:
                                    pe.wait_ge(mod_copied, primed(h))
                                for k in range(KD):
                                    ins = nc.tensor.matmul(ps[:, MISC + BANK + 2 * q:MISC + BANK + 2 * q + 2], m.modw[:, q % 2, k, :],
                                                           m.ccol[:, k, :], start=(k == 0), stop=(k == KD - 1))
                                ins.then_inc(mod_used, 1)
                                q += 1

        @block.scalar
        def _(act):
            def split(h, b):
                act.wait_ge(raw_in[b % 3], 16 * per_slot[b % 3] * h + 16 * (b // 3 + 1))
                act.wait_ge(w_used, primed(NB * h + b - 2 if b >= 3 else NB * h))
                nc.scalar.activation(m.wH[:, b % 3, :], m.wraw[:, b % 3, :], ACT.Copy).then_inc(w_high, 1)

            with act.Fori(0, 2) as h:
                for b in range(3):
                    split(h, b)
                b = 3
                for u, (kind, j) in enumerate(seq):
                    src = ps[:, (u % 2) * SLOT:(u % 2) * SLOT + TOK]
                    act.wait_ge(unit_done, primed(U * h + u + 1))
                    if kind == "x":
                        act.wait_ge(y_ready, primed(HALF * h))
                        nc.scalar.activation(m.x[:, j, :], src, ACT.Identity, scale=colreg(m, "rg_conv_w", 2 * KR + j, HALF * h),
                                             bias=colreg(m, "rg_conv_b", j, HALF * h)).then_inc(x_mid, 1)
                    elif kind == "g":
                        act.wait_ge(y_ready, primed(HALF * h + j))
                        nc.scalar.activation(m.GG[:, :], src, ACT.Gelu_apprx_tanh).then_inc(g_ready, 1)
                        act.wait_ge(g_ready, HALF * h + j + 1)
                        act.nop().then_inc(psum_free[u % 2], 1)
                    else:
                        d = int(kind[1])
                        n = 2 * j + d
                        if kind[0] == "r":
                            if d == 0:
                                act.wait_ge(y_stored, primed(HALF * h + j))
                            else:
                                act.wait_ge(y_ready, primed(HALF * h + j))
                            nc.scalar.activation(m.TR[:, d, :], src, ACT.Tanh, scale=0.5,
                                                 bias=lrucol(m, 3, KR * d + j, HALF * h)).then_inc(tr_ready, 1)
                            act.wait_ge(tr_ready, 2 * HALF * h + n + 1)
                            act.nop().then_inc(psum_free[u % 2], 1)
                        else:
                            act.wait_ge(scans, primed(2 * HALF * h + n))
                            nc.scalar.activation(m.TI[:, :], src, ACT.Tanh, scale=0.5,
                                                 bias=lrucol(m, 4, KR * d + j, HALF * h)).then_inc(ti_ready, 1)
                            act.wait_ge(ti_ready, 2 * HALF * h + n + 1)
                            act.nop().then_inc(psum_free[u % 2], 1)
                            nc.scalar.activation(m.A[:, :], m.TR[:, d, :], ACT.Exp, scale=lrucol(m, 2, KR * d + j, HALF * h),
                                                 bias=lrucol(m, 2, KR * d + j, HALF * h)).then_inc(a_ready, 1)
                            act.wait_ge(a_ready, 2 * HALF * h + n + 1)
                            nc.scalar.activation(m.TR[:, d, :], m.TR[:, d, :], ACT.Tanh, scale=lrucol(m, 0, KR * d + j, HALF * h),
                                                 bias=lrucol(m, 0, KR * d + j, HALF * h)).then_inc(t2_ready, 1)
                            act.wait_ge(t2_ready, 2 * HALF * h + n + 1)
                            nc.scalar.activation(m.TR[:, d, :], m.TR[:, d, :], ACT.Sqrt).then_inc(sq_ready, 1)
                    if kind in "xg" and b < NB:
                        split(h, b)
                        b += 1

        @block.vector
        def _(dve):
            prime(dve, (w_ready, 1), (y_ready, 1), (scans, 1), (psum_free[0], 1), (psum_free[1], 1), (mod_copied, 1))

            def split(h, b):
                dve.wait_ge(w_high, NB * h + b + 1)
                nc.vector.tensor_tensor(m.wL[:, b % 3, :], m.wraw[:, b % 3, :], m.wH[:, b % 3, :].bitcast(F32), ALU.subtract).then_inc(w_ready, 1)

            with dve.Fori(0, 2) as h:
                for b in range(3):
                    split(h, b)
                b = 3
                to = Order(dve, taps_order, n_taps * HALF * h)
                do = Order(dve, dir_order, (2 * 3 + 1 + 1) * HALF * h)
                for u, (kind, j) in enumerate(seq):
                    s = u % 2
                    src = ps[:, s * SLOT:s * SLOT + TOK]
                    if kind == "x":
                        dve.wait_ge(x_mid, HALF * h + j + 1)
                        taps(nc, dve, to, m.x[:, j, :], src, [(-2, colreg(m, "rg_conv_w", j, HALF * h)),
                                                              (-1, colreg(m, "rg_conv_w", KR + j, HALF * h)),
                                                              (1, colreg(m, "rg_conv_w", 3 * KR + j, HALF * h))], TOK)
                        dve.nop().then_inc(x_ready, 1)
                        dve.nop().then_inc(psum_free[s], 1)
                    if kind in ("i0", "i1"):
                        d = int(kind[1])
                        n = 2 * j + d
                        dve.wait_ge(ti_ready, 2 * HALF * h + n + 1)
                        do(nc.vector.scalar_tensor_tensor(out=m.TI[:, :], in0=m.TI[:, :], scalar=1.0, in1=m.x[:, j, :], op0=ALU.add, op1=ALU.mult))
                        dve.wait_ge(sq_ready, 2 * HALF * h + n + 1)
                        do(nc.vector.scalar_tensor_tensor(out=m.TR[:, d, :], in0=m.A[:, :], scalar=1.0, in1=m.TR[:, d, :], op0=ALU.add, op1=ALU.mult))
                        do(nc.vector.tensor_tensor(m.TI[:, :], m.TI[:, :], m.TR[:, d, :], ALU.mult))
                        if d == 0:
                            do(nc.vector.tensor_tensor_scan(out=m.TR[:, 0, SEQ:TOK], data0=m.A[:, SEQ:TOK], data1=m.TI[:, SEQ:TOK],
                                                            initial=0.0, op0=ALU.mult, op1=ALU.add))
                            nc.vector.tensor_tensor_scan(out=m.TR[:, 0, 0:SEQ], data0=m.A[:, 0:SEQ], data1=m.TI[:, 0:SEQ],
                                                         initial=m.TR[:, 0, TOK - 1:TOK], op0=ALU.mult, op1=ALU.add).then_inc(scans, 1)
                        else:
                            nc.vector.tensor_tensor_scan(out=m.TR[:, 1, ::-1], data0=m.A[:, ::-1], data1=m.TI[:, ::-1],
                                                         initial=0.0, op0=ALU.mult, op1=ALU.add).then_inc(scans, 1)
                        dve.wait_ge(scans, primed(2 * HALF * h + n + 1))
                        if d == 1:
                            do(nc.vector.tensor_tensor(m.TR[:, 0, :], m.TR[:, 0, :], m.TR[:, 1, :], ALU.add))
                            dve.wait_ge(g_ready, HALF * h + j + 1)
                            nc.vector.tensor_tensor(m.TR[:, 0, :], m.TR[:, 0, :], m.GG[:, :], ALU.mult).then_inc(y_ready, 1)
                    if kind in "xg" and b < NB:
                        split(h, b)
                        b += 1
                dve.wait_ge(mod_used, primed(MH * h + MH))
                for s in range(2):
                    ins = nc.vector.tensor_tensor(m.mod[:, 0, s, ds(2 * KD + MH * h, MH)], ps[:, MISC + BANK + s:MISC + BANK + 2 * MH:2],
                                                  m.vec[:, ds(VEC_AT["mod_b"] + 2 * KD + MH * h, MH)], ALU.add)
                ins.then_inc(mod_copied, 1)
            dve.wait_ge(mod_copied, primed(2))
            for s in range(2):
                nc.vector.scalar_tensor_tensor(out=m.gain[:, 0, 1, s, :], in0=m.mod[:, 0, s, 4 * KD:5 * KD], scalar=1.0,
                                               in1=vcol(m, "norm2_g", 0, KD), op0=ALU.add, op1=ALU.mult)
                nc.vector.tensor_scalar(m.gate[:, s, :], m.mod[:, 0, s, 2 * KD:3 * KD], 0.5, None, ALU.mult)


def colreg(m, name, i, reg):
    return m.vec[:, ds(reg + (VEC_AT[name] + i), 1)]


def lrucol(m, row, i, reg):
    return m.lru[:, row, ds(reg + i, 1)]


def project(nc, m, l, w, K, ntok):
    sem, ps = m.sem, m.ps
    tag = f"p{l}_"
    y_in = [sem(tag + "y_in0"), sem(tag + "y_in1")]
    y_high, y_ready = sem(tag + "y_high"), sem(tag + "y_ready")
    w_raw = [sem(tag + "w_raw0"), sem(tag + "w_raw1")]
    w_high, w_ready, unit_done = sem(tag + "w_high"), sem(tag + "w_ready"), sem(tag + "unit_done")
    psum_free = [sem(tag + "psum_free0"), sem(tag + "psum_free1")]
    res_in = [sem(tag + f"res_in{k}") for k in range(KD)]
    wv = w.rearrange("(k p) n -> p k n", p=P)

    def yH(k):
        return m.zH[:, k, :] if k < KD else m.yH[:, k - KD, :]

    def yL(k):
        return m.zL[:, k, :] if k < KD else m.yL[:, k - KD, :]

    def unit(pe, s, first, wait_ready, wait_free):
        pe.wait_ge(w_ready, wait_ready)
        if wait_free is not None:
            pe.wait_ge(psum_free[s], wait_free)
        for k in range(K):
            if first:
                pe.wait_ge(y_ready, k + 1)
            for i, (wt, r) in enumerate(((m.oH, yH(k)), (m.oH, yL(k)), (m.oL, yH(k)))):
                for c, n in chunks(ntok):
                    ins = nc.tensor.matmul(ps[:, s * SLOT + c:s * SLOT + c + n], wt[:, s, k, :], r[:, c:c + n],
                                           start=(k == 0 and i == 0), stop=(k == K - 1 and i == 2))
        ins.then_inc(unit_done, 1)

    with nc.Block() as block:
        @block.sync
        def _(sp):
            for s in range(2):
                sp.dma_start(m.oraw[:, s, 0:K, :], wv[:, :, s * P:(s + 1) * P]).then_inc(w_raw[s], 16)
            for k in range(2):
                sp.dma_start(m.yraw[:, k, 0:ntok], m.yT[k][:, 0:ntok]).then_inc(y_in[k], 16)
            if l == 0:
                for k in range(KD):
                    sp.dma_start(m.res[:, k, :], m.xT[k]).then_inc(res_in[k], 16)
            for k in range(2, K):
                sp.wait_ge(y_ready, k - 1)
                sp.dma_start(m.yraw[:, k % 2, 0:ntok], m.yT[k][:, 0:ntok]).then_inc(y_in[k % 2], 16)
            with sp.Fori(1, KD // 2) as i:
                for s in range(2):
                    sp.wait_ge(w_ready, 2 * i + s - 1)
                    sp.dma_start(m.oraw[:, s, 0:K, :], wv[:, :, ds(2 * P * i + s * P, P)]).then_inc(w_raw[s], 16)

        @block.scalar
        def _(act):
            for s in range(2):
                act.wait_ge(w_raw[s], 16)
                nc.scalar.activation(m.oH[:, s, 0:K, :], m.oraw[:, s, 0:K, :], ACT.Copy).then_inc(w_high, 1)
            for k in range(K):
                act.wait_ge(y_in[k % 2], 16 * (k // 2 + 1))
                nc.scalar.activation(yH(k)[:, 0:ntok], m.yraw[:, k % 2, 0:ntok], ACT.Copy).then_inc(y_high, 1)
            with act.Fori(1, KD // 2) as i:
                for s in range(2):
                    act.wait_ge(w_raw[s], 16 * i + 16)
                    act.wait_ge(unit_done, 2 * i + s - 1)
                    nc.scalar.activation(m.oH[:, s, 0:K, :], m.oraw[:, s, 0:K, :], ACT.Copy).then_inc(w_high, 1)

        @block.tensor
        def _(pe):
            for s in range(2):
                unit(pe, s, s == 0, s + 1, None)
            with pe.Fori(1, KD // 2) as i:
                for s in range(2):
                    unit(pe, s, False, 2 * i + s + 1, i)

        @block.vector
        def _(dve):
            def w_low(s, ready):
                dve.wait_ge(w_high, ready)
                nc.vector.tensor_tensor(m.oL[:, s, 0:K, :], m.oraw[:, s, 0:K, :], m.oH[:, s, 0:K, :].bitcast(F32), ALU.subtract).then_inc(w_ready, 1)

            def add(s, tile, done):
                dve.wait_ge(unit_done, done)
                mt = ds(tile, 1)
                for g, (a, b) in enumerate(segs(ntok)):
                    gt = m.gate[:, g, mt] if l == 0 else m.mod[:, l, g, ds(tile + 2 * KD, 1)]
                    r = m.res[:, mt, a:b].rearrange("p a t -> p (a t)")
                    ins = nc.vector.scalar_tensor_tensor(out=r, in0=ps[:, s * SLOT + a:s * SLOT + b], scalar=gt, in1=r, op0=ALU.mult, op1=ALU.add)
                ins.then_inc(psum_free[s], 1)

            for s in range(2):
                w_low(s, s + 1)
            for k in range(K):
                dve.wait_ge(y_high, k + 1)
                nc.vector.tensor_tensor(yL(k)[:, 0:ntok], m.yraw[:, k % 2, 0:ntok], yH(k)[:, 0:ntok].bitcast(F32), ALU.subtract).then_inc(y_ready, 1)
            if l == 0:
                for k in range(KD):
                    dve.wait_ge(res_in[k], 16)
            with dve.Fori(0, KD // 2 - 1) as i:
                for s in range(2):
                    add(s, 2 * i + s, 2 * i + s + 1)
                    w_low(s, 2 * i + s + 3)
            for s in range(2):
                add(s, KD - 2 + s, KD - 1 + s)


def ffn(nc, m, l, ntok):
    t, sem, ps = m.t, m.sem, m.ps
    tag = f"f{l}_"
    raw_in = [sem(tag + f"raw_in{i}") for i in range(3)]
    w_high, w_ready, w_used = sem(tag + "w_high"), sem(tag + "w_ready"), sem(tag + "w_used")
    unit_done, psum_free = sem(tag + "unit_done"), [sem(tag + "psum_free0"), sem(tag + "psum_free1")]
    mid, taps_order, g_conv, v_conv = sem(tag + "mid"), sem(tag + "taps_order"), sem(tag + "g_conv"), sem(tag + "v_conv")
    silu_done, h_full, h_high, h_ready = [sem(tag + n) for n in ("silu_done", "h_full", "h_high", "h_ready")]
    with_mod = l == 0
    mod_in, mod_used, mod_copied = [sem(tag + "mod_in0"), sem(tag + "mod_in1")], sem(tag + "mod_used"), sem(tag + "mod_copied")
    up = t["ffn_w_up"][l].rearrange("(k p) n -> p k n", p=P)
    down = t["ffn_w_down"][l].rearrange("(k p) n -> k p n", p=P)
    mod_w = t["mod_w"][1].rearrange("(k p) n -> p k n", p=P)
    NG = KF // 2
    ns = len(segs(ntok))
    HEAD = [("g", 0), ("v", 0), ("g", 1), ("v", 1)]
    BODY = [("g", 0), ("d", 0), ("v", 0), ("g", 1), ("v", 1)]
    TAIL = [("d", 0)]
    MPG = 4
    MOD_HEAD = N_MOD - MPG * (NG - 1)

    def program(eng, group):
        group(HEAD, 0, 0, 0, True)
        with eng.Fori(1, NG - 1) as i:
            group(BODY, i, 6 * i - 2, 12 * i - 8, False)
        group(BODY, NG - 1, 6 * (NG - 1) - 2, 12 * (NG - 1) - 8, False)
        group(TAIL, NG, 6 * NG - 2, 12 * NG - 8, False)

    def slot(first, k):
        return (k if first else k + 1) % 3

    def raw_count(first, i, k):
        if first:
            return 16 * (k // 3 + 1)
        s = (k + 1) % 3
        before = 2 if s == 0 else 1
        return 32 * i - 32 + 16 * before + 16 * ((k - (s - 1) % 3) // 3 + 1)

    def block_list(part):
        out = []
        for kind, j in part:
            out += [("d", 0), ("d", 1)] if kind == "d" else [(kind, j)]
        return out

    with nc.Block() as block:
        @block.sync
        def _(sp):
            def group(part, i, b0, u0, first):
                for k, (kind, j) in enumerate(block_list(part)):
                    s = slot(first, k)
                    if not (first and k < 3):
                        sp.wait_ge(w_ready, b0 + k - 2)
                    if kind == "d":
                        src = down[ds(2 * i - 2 + j, 1)].rearrange("a p n -> (a p) n")
                        sp.dma_start(m.wraw[:, s, :], src).then_inc(raw_in[s], 16)
                    else:
                        col = (0 if kind == "g" else D_FF) + P * j
                        sp.dma_start(m.wraw[:, s, :].rearrange("p (k n) -> p k n", k=KD), up[:, :, ds(2 * P * i + col, P)]).then_inc(raw_in[s], 16)
            program(sp, group)

        if with_mod:
            @block.gpsimd
            def _(gp):
                def group(part, i, b0, u0, first):
                    if part is TAIL:
                        return
                    for q in range(MOD_HEAD if first else MPG):
                        if first:
                            if q >= 2:
                                gp.wait_ge(mod_used, q - 1)
                            tile = q
                        else:
                            gp.wait_ge(mod_used, MPG * i + (MOD_HEAD - MPG + q - 1))
                            tile = MPG * i + (MOD_HEAD - MPG + q)
                        gp.dma_start(m.modw[:, q % 2, :, :], mod_w[:, :, ds(tile * P, P)]).then_inc(mod_in[q % 2], 16)
                program(gp, group)

        @block.tensor
        def _(pe):
            def group(part, i, b0, u0, first):
                k = u = 0
                for kind, j in part:
                    if kind != "d":
                        s = u % 2
                        if not (first and u < 2):
                            pe.wait_ge(psum_free[s], free(first, i, u))
                        pe.wait_ge(w_ready, b0 + k + 1)
                        wH, wL = m.wH[:, slot(first, k), :], m.wL[:, slot(first, k), :]
                        product(nc, ps, s, ntok, lambda n: wH[:, n * P:(n + 1) * P], lambda n: wL[:, n * P:(n + 1) * P],
                                lambda n: m.zH[:, n, :], lambda n: m.zL[:, n, :], KD).then_inc(unit_done, 1)
                        pe.wait_ge(unit_done, u0 + u + 1)
                        pe.nop().then_inc(w_used, 1)
                        u += 1
                        k += 1
                    else:
                        pe.wait_ge(w_ready, b0 + k + 2)
                        pe.wait_ge(h_ready, 2 * i)
                        for mt in range(KD):
                            s = u % 2
                            pe.wait_ge(psum_free[s], free(first, i, u))
                            product(nc, ps, s, ntok, lambda n: m.wH[:, slot(first, k + n), mt * P:(mt + 1) * P],
                                    lambda n: m.wL[:, slot(first, k + n), mt * P:(mt + 1) * P],
                                    lambda n: m.hH[:, n, :], lambda n: m.hL[:, n, :], 2).then_inc(unit_done, 1)
                            u += 1
                        pe.wait_ge(unit_done, u0 + u)
                        pe.nop().then_inc(w_used, 2)
                        k += 2
                if with_mod and part is not TAIL:
                    n = MOD_HEAD if first else MPG
                    for q in range(n):
                        if first:
                            pe.wait_ge(mod_in[q % 2], 16 * (q // 2 + 1))
                        else:
                            pe.wait_ge(mod_in[q % 2], (16 * MPG // 2) * i + (16 * (MOD_HEAD - MPG) // 2 + 16 * (q // 2 + 1)))
                            if q == 0:
                                pe.wait_ge(mod_copied, i)
                        for kk in range(KD):
                            ins = nc.tensor.matmul(ps[:, MISC + BANK + 2 * q:MISC + BANK + 2 * q + 2], m.modw[:, q % 2, kk, :], m.ccol[:, kk, :],
                                                   start=(kk == 0), stop=(kk == KD - 1))
                        ins.then_inc(mod_used, 1)

            def free(first, i, u):
                return u // 2 if first else 6 * i + (u // 2 - 4)
            program(pe, group)

        @block.scalar
        def _(act):
            def split(first, i, b0, k, n=1):
                for k in range(k, k + n):
                    s = slot(first, k)
                    act.wait_ge(raw_in[s], raw_count(first, i, k))
                    if not (first and k < 3):
                        act.wait_ge(w_used, b0 + k - 2)
                    nc.scalar.activation(m.wH[:, s, :], m.wraw[:, s, :], ACT.Copy).then_inc(w_high, 1)

            def group(part, i, b0, u0, first):
                if first:
                    split(True, 0, 0, 0, 3)
                k = u = 0
                for kind, j in part:
                    if kind != "d":
                        src = ps[:, (u % 2) * SLOT:(u % 2) * SLOT + ntok]
                        act.wait_ge(unit_done, u0 + u + 1)
                        dst = m.G if kind == "g" else m.V
                        act.wait_ge(h_ready, 2 * i + j)
                        col = 2 * i + ((0 if kind == "g" else KF) + j)
                        nc.scalar.activation(dst[:, 0:ntok], src, ACT.Identity, scale=fcol(m, l, 1, col), bias=fcol(m, l, 3, col)).then_inc(mid, 1)
                        after(first, i, b0, k + 3, part)
                        if kind == "g":
                            act.wait_ge(g_conv, 2 * i + j + 1)
                            nc.scalar.activation(m.G[:, 0:ntok], m.G[:, 0:ntok], ACT.Silu).then_inc(silu_done, 1)
                        else:
                            act.wait_ge(h_full, 2 * i + j + 1)
                            nc.scalar.activation(m.hH[:, j, 0:ntok], m.V[:, 0:ntok], ACT.Copy).then_inc(h_high, 1)
                        u += 1
                        k += 1
                    elif part is BODY:
                        after(first, i, b0, k + 3, part)
                        after(first, i, b0, k + 4, part)
                        u += 8
                        k += 2

            def after(first, i, b0, k, part):
                if isinstance(i, int) and i == NG - 1 and k >= 8:
                    return
                split(first, i, b0, k)
            program(act, group)

        @block.vector
        def _(dve):
            def split(first, i, b0, k, n=1):
                for k in range(k, k + n):
                    s = slot(first, k)
                    dve.wait_ge(w_high, b0 + k + 1)
                    nc.vector.tensor_tensor(m.wL[:, s, :], m.wraw[:, s, :], m.wH[:, s, :].bitcast(F32), ALU.subtract).then_inc(w_ready, 1)

            def after(first, i, b0, k):
                if isinstance(i, int) and i == NG - 1 and k >= 8:
                    return
                split(first, i, b0, k)

            def group(part, i, b0, u0, first):
                if first:
                    split(True, 0, 0, 0, 3)
                k = u = 0
                order = Order(dve, taps_order, 4 * (2 * ns) * i)
                for kind, j in part:
                    s = u % 2
                    if kind != "d":
                        src = ps[:, s * SLOT:s * SLOT + ntok]
                        dst = (m.G if kind == "g" else m.V)[:, 0:ntok]
                        dve.wait_ge(mid, u_mid(first, i, part, kind, j))
                        col = 2 * i + ((0 if kind == "g" else KF) + j)
                        taps(nc, dve, order, dst, src, [(-1, fcol(m, l, 0, col)), (1, fcol(m, l, 2, col))], ntok)
                        dve.nop().then_inc(psum_free[s], 1)
                        dve.nop().then_inc(g_conv if kind == "g" else v_conv, 1)
                        if kind == "v":
                            dve.wait_ge(silu_done, 2 * i + j + 1)
                            nc.vector.tensor_tensor(dst, dst, m.G[:, 0:ntok], ALU.mult).then_inc(h_full, 1)
                        after(first, i, b0, k + 3)
                        if kind == "v":
                            dve.wait_ge(h_high, 2 * i + j + 1)
                            nc.vector.tensor_tensor(m.hL[:, j, 0:ntok], dst, m.hH[:, j, 0:ntok].bitcast(F32), ALU.subtract).then_inc(h_ready, 1)
                        u += 1
                        k += 1
                    else:
                        for mt in range(KD):
                            s = u % 2
                            dve.wait_ge(unit_done, u0 + u + 1)
                            if not (isinstance(i, int) and i < 2):
                                dve.wait_ge(psum_free[s], 6 * i + (u // 2 - 4))
                            for g, (a, b) in enumerate(segs(ntok)):
                                ins = nc.vector.scalar_tensor_tensor(out=m.res[:, mt, a:b], in0=ps[:, s * SLOT + a:s * SLOT + b],
                                                                     scalar=m.mod[:, l, g, 5 * KD + mt:5 * KD + mt + 1], in1=m.res[:, mt, a:b],
                                                                     op0=ALU.mult, op1=ALU.add)
                            ins.then_inc(psum_free[s], 1)
                            u += 1
                        if part is BODY:
                            after(first, i, b0, k + 3)
                            after(first, i, b0, k + 4)
                        k += 2
                if with_mod and part is not TAIL:
                    n = MOD_HEAD if first else MPG
                    dve.wait_ge(mod_used, n if first else MPG * i + MOD_HEAD)
                    at = 0 if first else MPG * i + (MOD_HEAD - MPG)
                    for g in range(2):
                        ins = nc.vector.tensor_tensor(m.mod[:, 1, g, ds(at, n)], ps[:, MISC + BANK + g:MISC + BANK + 2 * n:2],
                                                      m.vec[:, ds(at + (VEC_AT["mod_b"] + N_MOD), n)], ALU.add)
                    ins.then_inc(mod_copied, 1)

            def u_mid(first, i, part, kind, j):
                return 4 * i + {("g", 0): 1, ("v", 0): 2, ("g", 1): 3, ("v", 1): 4}[(kind, j)]
            program(dve, group)
            if with_mod:
                dve.wait_ge(mod_copied, NG)
                for which in range(2):
                    for g in range(2):
                        sc = 3 * which * KD + KD
                        nc.vector.scalar_tensor_tensor(out=m.gain[:, 1, which, g, :], in0=m.mod[:, 1, g, sc:sc + KD], scalar=1.0,
                                                       in1=vcol(m, "norm1_g" if which == 0 else "norm2_g", KD, KD), op0=ALU.add, op1=ALU.mult)


def fcol(m, l, row, col):
    at = VEC_AT["ffn_conv_b"] + l * 2 * KF if row == 3 else VEC_AT["ffn_conv_w"] + (l * 3 + row) * 2 * KF
    return m.vec[:, ds(col + at, 1)]


def attention(nc, m):
    t, sem, ps = m.t, m.sem, m.ps
    raw_in = [sem(f"na_raw_in{i}") for i in range(3)]
    w_high, w_ready, w_used = sem("na_w_high"), sem("na_w_ready"), sem("na_w_used")
    qkv_done, q_zero, q_ready, k_ready, vT_ready, v_T, v_ready = [sem("na_" + n) for n in ("qkv_done", "q_zero", "q_ready", "k_ready", "vT_ready", "v_T", "v_ready")]
    bias_in, bias_ready = sem("na_bias_in"), sem("na_bias_ready")
    s_done, s_biased, negmax, exp_done, recip, p_ready = [sem("na_" + n) for n in ("s_done", "s_biased", "negmax", "exp_done", "recip", "p_ready")]
    t_done, pT_ready, o_done, o_ready, o_out = [sem("na_" + n) for n in ("t_done", "pT_ready", "o_done", "o_ready", "o_out")]
    o_stored = sem("na_o_stored")
    NP = KD
    w_in = t["na_w_in"][0].rearrange("(k p) n -> p k n", p=P)
    geo = []
    for r in range(ROWS):
        rs = min(max(r - NA_KR // 2, 0), ROWS - NA_KR)
        geo.append((rs, rs - r + NA_KR - 1))

    def program(eng, group):
        with eng.Fori(0, NP - 1) as i:
            group(i, False)
        group(NP - 1, True)

    def sbank(r):
        return (r % 2) * SLOT

    def obank(r):
        return (r % 2) * SLOT + 2 * BANK

    with nc.Block() as block:
        @block.sync
        def _(sp):
            def group(i, last):
                for k in range(3):
                    sp.wait_ge(w_ready, primed(3 * i))
                    sp.dma_start(m.wraw[:, k, :].rearrange("p (k n) -> p k n", k=KD), w_in[:, :, ds(P * i + D * k, P)]).then_inc(raw_in[k], 16)
                sp.wait_ge(s_biased, primed(ROWS * i))
                sp.dma_start(m.bias[:, :, :], m.biasT[ds(2 * i, 2)].rearrange("h q r c -> (h q) r c")).then_inc(bias_in, 16)
            program(sp, group)

        @block.gpsimd
        def _(gp):
            def group(i, last):
                gp.wait_ge(bias_in, 16 * i + 16)
                nc.gpsimd.tensor_tensor(m.bias[:, :, :], m.bias[:, :, :], m.mask[:, :].unsqueeze(1).to_broadcast([P, 15, GW]), ALU.add).then_inc(bias_ready, 1)
                gp.wait_ge(o_ready, primed(ROWS * i + ROWS))
                gp.dma_start(m.yT[ds(i, 1)].rearrange("a p t -> (a p) t")[:, 0:SEQ], m.oT[:, :]).then_inc(o_out, 16)
                gp.wait_ge(o_out, 16 * i + 16)
                gp.nop().then_inc(o_stored, 1)
            prime(gp, (o_stored, 1))
            nc.gpsimd.memset(m.qbd[:, :, :], 0.0).then_inc(q_zero, 1)
            program(gp, group)

        @block.tensor
        def _(pe):
            prime(pe, (w_used, 1), (o_done, 1))

            def scores(i, r):
                if r >= 2:
                    pe.wait_ge(s_biased, primed(ROWS * i + r - 1))
                rs, _ = geo[r]
                nc.tensor.matmul(ps[:, sbank(r):sbank(r) + WIN], m.qbd[:, r, :], m.kT[:, rs * GW:rs * GW + WIN], start=True, stop=True)
                nc.tensor.matmul(ps[:, sbank(r) + WIN:sbank(r) + KEYS], m.qbd[:, r, :], m.kT[:, SEQ:TOK], start=True, stop=True).then_inc(s_done, 1)

            def turn(i, r):
                pe.wait_ge(p_ready, ROWS * i + r + 1)
                pe.wait_ge(pT_ready, primed(ROWS * i + r))
                for c in range(KEYS // P):
                    ins = nc.tensor.transpose(ps[:, MISC + c * P:MISC + (c + 1) * P], m.S[:, r % 2, c * P:(c + 1) * P], m.ident[:, :])
                ins.then_inc(t_done, 1)

            def values(i, r):
                pe.wait_ge(pT_ready, primed(ROWS * i + r + 1))
                if r >= 2:
                    pe.wait_ge(o_ready, primed(ROWS * i + r - 1))
                rs, _ = geo[r]
                for c in range(KEYS // P):
                    if c >= WIN // P:
                        v = m.v0[:, SEQ // P + c - WIN // P, :]
                    else:
                        v = (m.v1 if rs % 2 else m.v0)[:, rs // 2 + c, :]
                    ins = nc.tensor.matmul(ps[:, obank(r):obank(r) + P], v, m.pT[:, r % 2, c * P:(c + 1) * P], start=(c == 0), stop=(c == KEYS // P - 1))
                ins.then_inc(o_done, 1)

            def group(i, last):
                pe.wait_ge(o_ready, primed(ROWS * i))
                pe.wait_ge(s_biased, primed(ROWS * i))
                for k in range(3):
                    pe.wait_ge(w_ready, primed(3 * i + k + 1))
                    if k == 2:
                        pe.wait_ge(q_ready, 2 * i + 2)
                    wH, wL = m.wH[:, k, :], m.wL[:, k, :]
                    product(nc, ps, k % 2, SEQ if k == 0 else TOK, lambda n: wH[:, n * P:(n + 1) * P], lambda n: wL[:, n * P:(n + 1) * P],
                            lambda n: m.zH[:, n, :], lambda n: m.zL[:, n, :], KD).then_inc(qkv_done, 1)
                    pe.wait_ge(qkv_done, 3 * i + k + 1)
                    pe.nop().then_inc(w_used, 1)
                pe.wait_ge(k_ready, i + 1)
                pe.wait_ge(vT_ready, i + 1)
                for c in range(TOK // P):
                    ins = nc.tensor.transpose(ps[:, SLOT + c * P:SLOT + (c + 1) * P], m.vT[:, c * P:(c + 1) * P], m.ident[:, :])
                ins.then_inc(v_T, 1)
                for c in range(SEQ // P - 1):
                    ins = nc.tensor.transpose(ps[:, c * P:(c + 1) * P], m.vT[:, c * P + GW:(c + 1) * P + GW], m.ident[:, :])
                ins.then_inc(v_T, 1)
                pe.wait_ge(v_ready, 2 * i + 2)
                scores(i, 0)
                scores(i, 1)
                for r in range(ROWS):
                    if r + 2 < ROWS and r >= 1:
                        scores(i, r + 1)
                    if r >= 1:
                        values(i, r - 1)
                    turn(i, r)
                    if r == ROWS - 2:
                        scores(i, r + 1)
                values(i, ROWS - 1)
            program(pe, group)

        @block.scalar
        def _(act):
            prime(act, (pT_ready, 1))

            def split(i, k):
                act.wait_ge(raw_in[k], 16 * i + 16)
                act.wait_ge(w_used, primed(3 * i))
                nc.scalar.activation(m.wH[:, k, :], m.wraw[:, k, :], ACT.Copy).then_inc(w_high, 1)

            def group(i, last):
                act.wait_ge(qkv_done, 3 * i + 1)
                act.wait_ge(o_done, primed(ROWS * i))
                for h in range(2):
                    p0 = h * DH
                    nc.scalar.activation(m.qbd[p0:p0 + DH, :, p0:p0 + DH], ps[p0:p0 + DH, 0:SEQ].rearrange("p (r c) -> p r c", c=GW),
                                         ACT.Copy, scale=DH ** -0.5).then_inc(q_ready, 1)
                act.wait_ge(qkv_done, 3 * i + 2)
                nc.scalar.activation(m.kT[:, :], ps[:, SLOT:SLOT + TOK], ACT.Copy).then_inc(k_ready, 1)
                act.wait_ge(v_T, 2 * i + 1)
                nc.scalar.activation(m.v0[:, :, :], ps[:, SLOT:SLOT + TOK].rearrange("p (c f) -> p c f", f=P), ACT.Copy).then_inc(v_ready, 1)
                for r in range(ROWS + 1):
                    if r < ROWS:
                        act.wait_ge(negmax, ROWS * i + r + 1)
                        nc.scalar.activation(m.S[:, r % 2, :], m.S[:, r % 2, :], ACT.Exp, bias=m.rowstat[:, r % 2, 0:1],
                                             accum_out=m.rowstat[:, r % 2, 1:2]).then_inc(exp_done, 1)
                    if r >= 1:
                        act.wait_ge(t_done, ROWS * i + r)
                        if r >= 3:
                            act.wait_ge(o_done, primed(ROWS * i + r - 2))
                        nc.scalar.activation(m.pT[:, (r - 1) % 2, :], ps[:, MISC:MISC + KEYS], ACT.Copy).then_inc(pT_ready, 1)
                    if 4 <= r < 7 and not last:
                        split(i + 1, r - 4)
            act.wait_ge(q_zero, 1)
            for k in range(3):
                split(0, k)
            program(act, group)

        @block.vector
        def _(dve):
            prime(dve, (w_ready, 1), (s_biased, 1), (o_ready, 1))

            def split(i, k):
                dve.wait_ge(w_high, 3 * i + k + 1)
                nc.vector.tensor_tensor(m.wL[:, k, :], m.wraw[:, k, :], m.wH[:, k, :].bitcast(F32), ALU.subtract).then_inc(w_ready, 1)

            def out(i, r):
                dve.wait_ge(o_done, primed(ROWS * i + r + 1))
                for h in range(2):
                    p0 = h * DH
                    ins = nc.vector.tensor_copy(m.oT[p0:p0 + DH, r * GW:(r + 1) * GW], ps[p0:p0 + DH, obank(r) + p0:obank(r) + p0 + DH])
                ins.then_inc(o_ready, 1)

            def group(i, last):
                dve.wait_ge(qkv_done, 3 * i + 3)
                nc.vector.tensor_copy(m.vT[:, :], ps[:, 0:TOK]).then_inc(vT_ready, 1)
                dve.wait_ge(v_T, 2 * i + 2)
                nc.vector.tensor_copy(m.v1[:, :, :], ps[:, 0:SEQ - P].rearrange("p (c f) -> p c f", f=P)).then_inc(v_ready, 1)
                dve.wait_ge(bias_ready, i + 1)
                dve.wait_ge(o_stored, primed(i))
                for r in range(ROWS + 1):
                    if r < ROWS:
                        q = r % 2
                        dve.wait_ge(s_done, ROWS * i + r + 1)
                        if r >= 2:
                            dve.wait_ge(t_done, ROWS * i + r - 1)
                        dr = geo[r][1]
                        nc.vector.tensor_copy(m.S[:, q, WIN:KEYS], ps[:, sbank(r) + WIN:sbank(r) + KEYS])
                        nc.vector.tensor_tensor(m.S[:, q, 0:WIN], ps[:, sbank(r):sbank(r) + WIN],
                                                m.bias[:, dr:dr + NA_KR, :].rearrange("p r c -> p (r c)"), ALU.add).then_inc(s_biased, 1)
                        dve.wait_ge(s_biased, primed(ROWS * i + r + 1))
                        nc.vector.tensor_reduce(m.rowstat[:, q, 0:1], m.S[:, q, :], AX_X, ALU.max, negate=True).then_inc(negmax, 1)
                    if r >= 2:
                        out(i, r - 2)
                    if r < ROWS:
                        dve.wait_ge(exp_done, ROWS * i + r + 1)
                        nc.vector.reciprocal(m.rowstat[:, q, 2:3], m.rowstat[:, q, 1:2]).then_inc(recip, 1)
                        dve.wait_ge(recip, ROWS * i + r + 1)
                        nc.vector.tensor_scalar(m.S[:, q, :], m.S[:, q, :], m.rowstat[:, q, 2:3], None, ALU.mult).then_inc(p_ready, 1)
                    if 4 <= r < 7 and not last:
                        split(i + 1, r - 4)
                out(i, ROWS - 1)
            for k in range(3):
                split(0, k)
            program(dve, group)


def final(nc, m):
    st = norm_stats(nc, m, "fin", SEQ)
    ps = m.ps
    normed, turned, low_half, high_half = [m.sem("fin_" + n) for n in ("normed", "turned", "low_half", "high_half")]
    stored = [m.sem("fin_stored0"), m.sem("fin_stored1")]

    with nc.Block() as block:
        @block.sync
        def _(sp):
            for i in range(SEQ // P):
                sp.wait_ge(low_half, i + 1)
                sp.wait_ge(high_half, i + 1)
                sp.dma_start(m.out[0, i * P:(i + 1) * P, :], m.outT[:, i % 2, :]).then_inc(stored[i % 2], 16)
            for s in range(2):
                sp.wait_ge(stored[s], 16 * (SEQ // P // 2))

        @block.scalar
        def _(act):
            st.act(act)
            for i in range(SEQ // P):
                act.wait_ge(turned, i + 1)
                if i >= 2:
                    act.wait_ge(stored[i % 2], 16 * (i // 2))
                o = (i % 2) * SLOT
                nc.scalar.activation(m.outT[:, i % 2, 0:BANK], ps[:, o:o + BANK], ACT.Copy).then_inc(low_half, 1)

        @block.tensor
        def _(pe):
            st.pe(pe)
            pe.wait_ge(normed, KD)
            for i in range(SEQ // P):
                if i >= 2:
                    pe.wait_ge(low_half, i - 1)
                    pe.wait_ge(high_half, i - 1)
                o = (i % 2) * SLOT
                for k in range(KD):
                    ins = nc.tensor.transpose(ps[:, o + k * P:o + (k + 1) * P], m.res[:, k, i * P:(i + 1) * P], m.ident[:, :])
                ins.then_inc(turned, 1)

        @block.vector
        def _(dve):
            st.dve(dve)
            for k in range(KD):
                nc.vector.scalar_tensor_tensor(out=m.res[:, k, 0:SEQ], in0=m.res[:, k, 0:SEQ], scalar=vcol(m, "final_g", k),
                                               in1=m.rstd[:, 0:SEQ], op0=ALU.mult, op1=ALU.mult).then_inc(normed, 1)
            for i in range(SEQ // P):
                dve.wait_ge(turned, i + 1)
                if i >= 2:
                    dve.wait_ge(stored[i % 2], 16 * (i // 2))
                o = (i % 2) * SLOT
                nc.vector.tensor_copy(m.outT[:, i % 2, BANK:D], ps[:, o + BANK:o + D]).then_inc(high_half, 1)


_INS = ['x', 'c', 'ctx', 'c_ctx', 'mod_w', 'mod_b', 'norm1_g', 'norm2_g',
        'rg_w_in', 'rg_conv_w', 'rg_conv_b', 'rg_wa', 'rg_ba', 'rg_wx', 'rg_bx', 'rg_lam', 'rg_w_out',
        'na_w_in', 'na_rpb', 'na_w_out', 'ffn_w_up', 'ffn_conv_w', 'ffn_conv_b', 'ffn_w_down', 'final_g']
_OUTS = [((1, 1024, 1024), 'float32')]


def kernel(**inputs):
    import numpy as _np
    import concourse.bacc as _bacc
    from concourse import mybir as _mybir
    from concourse.bass_utils import run_bass_kernel_spmd as _run

    nc = _bacc.Bacc("TRN2", target_bir_lowering=False, num_devices=1)
    arrays, args = {}, {}
    for name in _INS:
        a = _np.ascontiguousarray(inputs[name])
        arrays[f"in_{name}_dram"] = a
        args[name] = nc.dram_tensor(f"in_{name}_dram", a.shape, _mybir.dt.from_np(a.dtype), kind="ExternalInput").ap()
    outs = [nc.dram_tensor(f"out_{i}_dram", shape, _mybir.dt.from_np(_np.dtype(dtype)), kind="ExternalOutput").ap()
            for i, (shape, dtype) in enumerate(_OUTS)]
    build(nc, args, outs[0])
    r = _run(nc, [arrays], core_ids=[0])
    return tuple(r.results[0][f"out_{i}_dram"] for i in range(len(_OUTS)))[0]
```

```python
from contextlib import ExitStack

import concourse.bass as bass
from concourse import mybir

F32 = mybir.dt.float32
F32R = mybir.dt.float32r
ALU = mybir.AluOpType
ACT = mybir.ActivationFunctionType
AX_X = mybir.AxisListType.X
ds = bass.ds

P = 128
D = 1024
SEQ = 1024
CTX = 256
TOK = SEQ + CTX
KD = D // P
D_RNN = 1280
KR = D_RNN // P
RG_BW = 160
HALF = KR // 2
D_FF = 2816
KF = D_FF // P
N_MOD = 6 * KD
HEADS = 16
DH = 64
ROWS = SEQ // 64
GW = 64
NA_KR, NA_KC = 8, 16
WIN = NA_KR * GW
KEYS = WIN + CTX
EPS = 1e-6
MASKED = -1.0e30
BANK = 512
SLOT = 3 * BANK
MISC = 2 * SLOT

LAT = (0, SEQ)
CTXS = (SEQ, TOK)
STOP = 99


def chunks(ntok):
    return [(c, min(BANK, ntok - c)) for c in range(0, ntok, BANK)]


def segs(ntok):
    return [LAT] if ntok == SEQ else [LAT, CTXS]


def gate_pairs():
    out = []
    for mt in range(HALF):
        b0, b1 = mt * P // RG_BW, (mt * P + P - 1) // RG_BW
        k0, k1 = b0 * RG_BW // P, (b1 * RG_BW + RG_BW - 1) // P
        out += [(mt, kt) for kt in range(k0, k1 + 1)]
    return out


PAIRS = gate_pairs()


def gate_rects():
    out = []
    for p, (mt, kt) in enumerate(PAIRS):
        for b in range(4):
            r0, r1 = max(kt * P, b * RG_BW), min(kt * P + P, (b + 1) * RG_BW)
            c0, c1 = max(mt * P, b * RG_BW), min(mt * P + P, (b + 1) * RG_BW)
            if r0 < r1 and c0 < c1:
                out.append((p, b, r0 - kt * P, r0 - b * RG_BW, r1 - r0, c0 - mt * P, c0 - b * RG_BW, c1 - c0))
    return out


RECTS = gate_rects()

VECS = [("mod_b", 2 * N_MOD), ("norm1_g", 2 * KD), ("norm2_g", 2 * KD), ("final_g", KD), ("c", KD), ("c_ctx", KD),
        ("rg_conv_w", 4 * KR), ("rg_conv_b", KR), ("rg_ba", 2 * KR), ("rg_bx", 2 * KR), ("rg_lam", 2 * KR),
        ("ffn_conv_w", 2 * 3 * 2 * KF), ("ffn_conv_b", 2 * 2 * KF)]
VEC_AT = {}
N_VEC = 0
for _name, _rows in VECS:
    VEC_AT[_name] = N_VEC
    N_VEC += _rows
VT = (N_VEC + P - 1) // P


def prime(eng, *sems):
    for s, n in sems:
        eng.nop().then_inc(s, n)


def primed(value, start=1):
    return value + start


class Bag:
    pass


class Order:

    def __init__(self, eng, sem, base=0):
        self.eng, self.sem, self.base, self.n = eng, sem, base, 0

    def __call__(self, ins):
        self.n += 1
        ins.then_inc(self.sem, 1)
        self.eng.wait_ge(self.sem, self.base + self.n)


class Plan:

    def __init__(self, nc, at):
        self.nc, self.at = nc, at

    def put(self, name, shape, dt=F32):
        n = 4
        for s in shape[1:]:
            n *= s
        t = self.nc.alloc_sbuf_tensor_at(name, shape, dt, offset=self.at)
        self.at += (n + 31) // 32 * 32
        return t

    def same_place(self):
        return Plan(self.nc, self.at)


def build(nc, t, out):
    es = ExitStack()
    m = Bag()
    m.t = t
    m.out = out

    phase_sems = []

    def sem(name):
        phase_sems.append(nc.alloc_semaphore(name))
        return phase_sems[-1]

    def run(phase, *args):
        phase(nc, m, *args)
        nc.clear_and_free_semaphores(list(phase_sems))
        phase_sems.clear()
        nc.all_engine_barrier()

    m.sem = sem
    m.xT = nc.dram_tensor("scratch_xT", [KD, P, TOK], F32).ap()
    m.yT = nc.dram_tensor("scratch_yT", [KR, P, TOK], F32).ap()
    m.rpbT = nc.dram_tensor("scratch_rpb", [HEADS, 15, 127], F32).ap()
    m.biasT = nc.dram_tensor("scratch_bias", [HEADS, GW, 15, GW], F32).ap()

    pl = Plan(nc, (nc.sbuf_base + 63) // 64 * 64)
    m.vec = pl.put("vec", [P, VT * P])
    m.ident = pl.put("ident", [P, P])
    m.ones = pl.put("ones", [P, P])
    m.eps = pl.put("eps", [P, 1])
    m.mod = pl.put("mod", [P, 2, 2, N_MOD])
    m.ccol = pl.put("ccol", [P, KD, 2])
    m.gain = pl.put("gain", [P, 2, 2, 2, KD])
    m.gate = pl.put("gate", [P, 2, KD])
    m.mask = pl.put("mask", [P, GW])
    m.root = pl.put("root", [P, TOK // P])
    m.lru = pl.put("lru", [P, 6, 2 * KR])
    modring_at = pl.at
    m.modw = pl.put("modw", [P, 2, KD, P])
    m.acc0 = Plan(nc, modring_at).put("acc0", [P, TOK])
    bp = Plan(nc, modring_at)
    m.bias = bp.put("bias", [P, 15, GW])
    ring_at = pl.at
    m.wraw = pl.put("wraw", [P, 3, D])
    m.wH = pl.put("wH", [P, 3, D], F32R)
    m.wL = pl.put("wL", [P, 3, D], F32R)
    m.S2 = Plan(nc, ring_at + 2 * D * 4).put("S2", [P, KEYS])
    op = Plan(nc, ring_at)
    m.oraw = op.put("oraw", [P, 2, KR, P])
    op.at = ring_at + 3 * D * 4
    m.oH = op.put("oH", [P, 2, KR, P], F32R)
    m.oL = op.put("oL", [P, 2, KR, P], F32R)
    z_at = pl.at
    m.zH = pl.put("zH", [P, KD, TOK], F32R)
    m.zLraw = Plan(nc, pl.at).put("zLraw", [P, KD, TOK])
    m.zL = pl.put("zL", [P, KD, TOK], F32R)
    zp = Plan(nc, z_at)
    m.xraw = zp.put("xraw", [P, TOK // P, D])
    m.vraw = zp.put("vraw", [P, VT, P])
    m.rpb = zp.put("rpb", [P, 2, 127])
    m.modpair = zp.put("modpair", [P, 4, KD, 2 * P])
    assert zp.at <= z_at + 2 * KD * TOK * 4
    zp = Plan(nc, z_at)
    m.outT = zp.put("outT", [P, 2, D])
    arena = pl.at

    a = Plan(nc, arena)
    m.res = a.put("res", [P, KD, TOK])
    w = a.same_place()
    m.diag = Plan(nc, w.at).put("diag", [P, TOK // P, P])
    m.sq = w.put("sq", [P, 2, TOK])
    w = a.same_place()
    w.put("sq_p", [P, 2, TOK])
    m.yH = w.put("yH", [P, KR - KD, TOK], F32R)
    m.yLraw = Plan(nc, w.at).put("yLraw", [P, KR - KD, TOK])
    m.yL = w.put("yL", [P, KR - KD, TOK], F32R)
    w = a.same_place()
    m.G = w.put("G", [P, TOK])
    m.V = w.put("V", [P, TOK])
    m.hH = w.put("hH", [P, 2, TOK], F32R)
    m.hL = w.put("hL", [P, 2, TOK], F32R)
    m.acc = w.put("acc", [P, TOK])
    w = a.same_place()
    m.qbd = w.put("qbd", [P, ROWS, P])
    m.kT = w.put("kT", [P, TOK])
    m.v0 = w.put("v0", [P, TOK // P, P])
    m.v1 = w.put("v1", [P, SEQ // P - 1, P])
    vt_at = w.at
    m.S = w.put("S", [P, 2, KEYS])
    m.vT = Plan(nc, vt_at).put("vT", [P, TOK])
    zp = Plan(nc, vt_at)
    m.na_ztmp = zp.put("na_ztmp", [P, 2, TOK])
    m.na_diag = zp.put("na_diag", [P, TOK // P, P])
    m.pT = w.put("pT", [P, 2, KEYS])
    m.oT = w.put("oT", [P, SEQ])
    w = Plan(nc, arena)
    m.x = w.put("xconv", [P, HALF, TOK])
    m.TR = w.put("TR", [P, 2, TOK])
    m.TI = w.put("TI", [P, TOK])
    m.A = w.put("A", [P, TOK])
    m.GG = w.put("GG", [P, TOK])
    w.at = max(w.at, arena + (KD + 2) * TOK * 4)
    m.gW = w.put("gW", [P, 4, len(PAIRS), P])
    sm = Plan(nc, nc.sbuf_usable_end // 32 * 32 - 64)
    m.rowstat = sm.put("rowstat", [P, 3, 4])

    m.ps = es.enter_context(nc.psum_tensor("ps", [P, 8 * BANK], F32))

    with es:
        run(setup)
        if STOP >= 2:
            run(rglru)
        if STOP >= 3:
            run(project, 0, m.t["rg_w_out"][0], KR, TOK)
        if STOP >= 4:
            run(ffn, 0, TOK)
        if STOP >= 5:
            run(attention)
            run(project, 1, m.t["na_w_out"][0], KD, SEQ)
            run(ffn, 1, SEQ)
        final(nc, m)


def vcol(m, name, i, n=1):
    at = VEC_AT[name] + i
    return m.vec[:, at:at + n]


def setup(nc, m):
    t, sem, ps = m.t, m.sem, m.ps
    x_in = [sem(f"su_x_in{i}") for i in range(TOK // P)]
    vec_in = sem("su_vec_in")
    rpb_zero, rpb_in, rpb_out = sem("su_rpb_zero"), sem("su_rpb_in"), sem("su_rpb_out")
    mod_in = [sem(f"su_mod_in{i}") for i in range(4)]
    mod_used = sem("su_mod_used")
    const, vec_T, vec_ready, c_ready = sem("su_const"), sem("su_vec_T"), sem("su_vec_ready"), sem("su_c_ready")
    xT_done, res_ready, spilled = sem("su_xT_done"), sem("su_res_ready"), sem("su_spilled")
    v_order, a_order, lru_ready = sem("su_v_order"), sem("su_a_order"), sem("su_lru")
    act_ln = sem("su_act_ln")
    sq_ready, acc_done = sem("su_sq_ready"), sem("su_acc_done")
    NT = TOK // P
    src = {"mod_b": t["mod_b"].rearrange("l (n p) -> (l n) p", p=P), "norm1_g": t["norm1_g"].rearrange("l (n p) -> (l n) p", p=P),
           "norm2_g": t["norm2_g"].rearrange("l (n p) -> (l n) p", p=P), "final_g": t["final_g"].rearrange("(n p) -> n p", p=P),
           "c": t["c"].rearrange("b (n p) -> (b n) p", p=P), "c_ctx": t["c_ctx"].rearrange("(n p) -> n p", p=P),
           "rg_conv_w": t["rg_conv_w"][0].rearrange("k (n p) -> (k n) p", p=P), "rg_conv_b": t["rg_conv_b"].rearrange("a (n p) -> (a n) p", p=P),
           "rg_ba": t["rg_ba"][0].rearrange("k (n p) -> (k n) p", p=P), "rg_bx": t["rg_bx"][0].rearrange("k (n p) -> (k n) p", p=P),
           "rg_lam": t["rg_lam"][0].rearrange("k (n p) -> (k n) p", p=P),
           "ffn_conv_w": t["ffn_conv_w"].rearrange("l k (n p) -> (l k n) p", p=P), "ffn_conv_b": t["ffn_conv_b"].rearrange("l (n p) -> (l n) p", p=P)}
    vec_dmas = []
    for name, rows in VECS:
        done = 0
        while done < rows:
            at = VEC_AT[name] + done
            k = min(rows - done, P - at % P)
            vec_dmas.append((at // P, at % P, k, src[name][done:done + k, :]))
            done += k

    def mod_weights(sp, q):
        sp.dma_start(m.modpair[:, q % 4, :, :], t["mod_w"][0].rearrange("(k p) n -> p k n", p=P)[:, :, 2 * q * P:2 * (q + 1) * P]).then_inc(mod_in[q % 4], 16)

    with nc.Block() as block:
        @block.sync
        def _(sp):
            for tile, row, k, s in vec_dmas:
                sp.dma_start(m.vraw[row:row + k, tile, :], s).then_inc(vec_in, 16)
            for q in range(4):
                mod_weights(sp, q)
            for i in range(NT):
                s = t["x"][0, i * P:(i + 1) * P, :] if i < SEQ // P else t["ctx"][0, i * P - SEQ:(i + 1) * P - SEQ, :]
                sp.dma_start(m.xraw[:, i, :], s).then_inc(x_in[i], 16)
            for q in range(4, KD):
                sp.wait_ge(mod_used, 2 * q - 6)
                mod_weights(sp, q)
            for f in range(KD):
                sp.wait_ge(res_ready, f + 1)
                sp.dma_start(m.xT[f], m.res[:, f, :]).then_inc(spilled, 16)
            sp.wait_ge(spilled, 16 * KD)

        @block.gpsimd
        def _(gp):
            mo = Order(gp, const)
            mo(nc.gpsimd.memset(m.ident[:, :], 0.0))
            mo(nc.gpsimd.affine_select(out=m.ident[:, :], in_=m.ident[:, :], compare_op=ALU.not_equal, fill=1.0, base=0,
                                       pattern=[[-1, P]], channel_multiplier=1))
            mo(nc.gpsimd.memset(m.ones[:, :], 1.0))
            mo(nc.gpsimd.memset(m.eps[:, :], EPS))
            mo(nc.gpsimd.memset(m.mask[:, :], 0.0))
            for h in range(2):
                pr = m.mask[h * 64:h * 64 + 64, :]
                lo = pr[:, 0:GW - NA_KC]
                mo(nc.gpsimd.affine_select(out=lo, in_=lo, compare_op=ALU.is_ge, fill=MASKED, base=NA_KC // 2,
                                           pattern=[[1, GW - NA_KC]], channel_multiplier=-1))
                hi = pr[:, NA_KC:GW]
                mo(nc.gpsimd.affine_select(out=hi, in_=hi, compare_op=ALU.is_gt, fill=MASKED, base=NA_KC // 2 - NA_KC,
                                           pattern=[[-1, GW - NA_KC]], channel_multiplier=1))
            nc.gpsimd.memset(m.rpb[:, :, :], 0.0).then_inc(rpb_zero, 1)
            gp.wait_ge(rpb_zero, 1)
            half = HEADS * 15 // 2
            gp.dma_start(m.rpb[0:half, :, 48:79], t["na_rpb"][0].rearrange("h r c -> (h r) c").rearrange("(p a) c -> p a c", a=2)).then_inc(rpb_in, 16)
            gp.wait_ge(rpb_in, 16)
            gp.dma_start(m.rpbT.rearrange("h r c -> (h r) c").rearrange("(p a) c -> p a c", a=2), m.rpb[0:half, :, :]).then_inc(rpb_out, 16)
            nc.gpsimd.memset(m.gW[:, :, :, :], 0.0)
            gp.wait_ge(rpb_out, 16)

        @block.tensor
        def _(pe):
            def modulation(tiles):
                for q in tiles:
                    pair = q // 2
                    pe.wait_ge(mod_in[pair % 4], 16 * (pair // 4 + 1))
                    for k in range(KD):
                        ins = nc.tensor.matmul(ps[:, MISC + BANK + 2 * q:MISC + BANK + 2 * q + 2],
                                               m.modpair[:, pair % 4, k, (q % 2) * P:(q % 2 + 1) * P], m.ccol[:, k, :],
                                               start=(k == 0), stop=(k == KD - 1))
                    ins.then_inc(mod_used, 1)

            pe.wait_ge(const, 2)
            pe.wait_ge(vec_in, 16 * len(vec_dmas))
            for i in range(VT):
                n = min(P, N_VEC - i * P)
                ins = nc.tensor.transpose(ps[:, MISC + i * P:MISC + i * P + n], m.vraw[0:n, i, :], m.ident[0:n, 0:n])
            ins.then_inc(vec_T, 1)
            pe.wait_ge(c_ready, 2)
            pe.wait_ge(vec_ready, 2)
            modulation(range(KD))
            for f in range(KD):
                s = f % 2
                if f >= 2:
                    pe.wait_ge(res_ready, f - 1)
                for i in range(NT):
                    if f == 0:
                        pe.wait_ge(x_in[i], 16)
                    ins = nc.tensor.transpose(ps[:, s * SLOT + i * P:s * SLOT + i * P + P], m.xraw[:, i, f * P:(f + 1) * P], m.ident[:, :])
                ins.then_inc(xT_done, 1)
                if f >= 2:
                    modulation([KD + f - 2])
            modulation(range(2 * KD - 2, 2 * KD))

        @block.scalar
        def _(act):
            act.wait_ge(vec_T, 1)
            nc.scalar.activation(m.vec[:, 0:BANK], ps[:, MISC:MISC + BANK], ACT.Copy).then_inc(vec_ready, 1)
            nc.scalar.activation(m.vec[:, BANK:N_VEC], ps[:, MISC + BANK:MISC + N_VEC], ACT.Copy).then_inc(vec_ready, 1)
            act.wait_ge(vec_ready, 2)
            for s, name in enumerate(("c", "c_ctx")):
                nc.scalar.activation(m.ccol[:, :, s], vcol(m, name, 0, KD), ACT.Silu).then_inc(c_ready, 1)
            for f in range(KD):
                act.wait_ge(res_ready, f + 1)
                if f >= 2:
                    act.wait_ge(acc_done, f - 1)
                nc.scalar.activation(m.sq[:, f % 2, :], m.res[:, f, :], ACT.Square).then_inc(sq_ready, 1)
            lam = vcol(m, "rg_lam", 0, 2 * KR)
            ao = Order(act, a_order)
            ao(nc.scalar.activation(m.lru[:, 0, :], lam, ACT.Abs))
            ao(nc.scalar.activation(m.lru[:, 0, :], m.lru[:, 0, :], ACT.Exp, scale=-1.0))
            act.wait_ge(lru_ready, 1)
            nc.scalar.activation(m.lru[:, 2, :], m.lru[:, 1, :], ACT.Ln).then_inc(act_ln, 1)
            act.wait_ge(act_ln, 1)
            nc.scalar.activation(m.lru[:, 3, :], m.lru[:, 2, :], ACT.Tanh, scale=0.5).then_inc(act_ln, 1)

        @block.vector
        def _(dve):
            vo = Order(dve, v_order)
            for f in range(KD):
                dve.wait_ge(xT_done, f + 1)
                nc.vector.tensor_copy(m.res[:, f, :], ps[:, (f % 2) * SLOT:(f % 2) * SLOT + TOK]).then_inc(res_ready, 1)
                if f == 1:
                    dve.wait_ge(sq_ready, f)
                    nc.vector.tensor_copy(m.acc0[:, :], m.sq[:, 0, :]).then_inc(acc_done, 1)
                if f >= 2:
                    dve.wait_ge(sq_ready, f)
                    dve.wait_ge(acc_done, f - 1)
                    nc.vector.tensor_tensor(m.acc0[:, :], m.acc0[:, :], m.sq[:, (f - 1) % 2, :], ALU.add).then_inc(acc_done, 1)
            lru_constants(nc, m, dve, vo, a_order, lru_ready, act_ln)
            dve.wait_ge(mod_used, 2 * KD)
            for s in range(2):
                vo(nc.vector.tensor_tensor(m.mod[:, 0, s, 0:2 * KD], ps[:, MISC + BANK + s:MISC + BANK + 4 * KD:2],
                                           vcol(m, "mod_b", 0, 2 * KD), ALU.add))
            for s in range(2):
                vo(nc.vector.scalar_tensor_tensor(out=m.gain[:, 0, 0, s, :], in0=m.mod[:, 0, s, KD:2 * KD], scalar=1.0,
                                                  in1=vcol(m, "norm1_g", 0, KD), op0=ALU.add, op1=ALU.mult))


def lru_constants(nc, m, dve, vo, a_order, lru_ready, act_ln):
    lam = vcol(m, "rg_lam", 0, 2 * KR)
    r = [m.lru[:, i, :] for i in range(6)]
    dve.wait_ge(a_order, 2)
    nc.vector.tensor_scalar(r[1], r[0], 1.0, None, ALU.add).then_inc(lru_ready, 1)
    dve.wait_ge(lru_ready, 1)
    dve.wait_ge(act_ln, 2)
    vo(nc.vector.tensor_scalar(r[4], r[3], -1.0, 1.0, ALU.mult, ALU.add))
    vo(nc.vector.reciprocal(r[4], r[4]))
    vo(nc.vector.scalar_tensor_tensor(out=r[3], in0=r[3], scalar=2.0, in1=r[4], op0=ALU.mult, op1=ALU.mult))
    vo(nc.vector.tensor_tensor(r[3], r[3], r[0], ALU.subtract))
    vo(nc.vector.reciprocal(r[1], r[1]))
    vo(nc.vector.tensor_tensor(r[3], r[3], r[1], ALU.mult))
    vo(nc.vector.tensor_tensor(r[2], r[2], r[3], ALU.subtract))
    vo(nc.vector.tensor_scalar(r[1], lam, -1.0, 0.0, ALU.mult, ALU.max))
    vo(nc.vector.tensor_tensor(r[5], r[1], r[2], ALU.add))
    vo(nc.vector.tensor_scalar(r[0], r[5], 2.0, None, ALU.mult))
    vo(nc.vector.tensor_scalar(r[1], r[5], 4.0, None, ALU.mult))
    vo(nc.vector.tensor_scalar(r[2], r[5], -4.0, None, ALU.mult))
    vo(nc.vector.tensor_scalar(r[3], vcol(m, "rg_ba", 0, 2 * KR), 0.5, None, ALU.mult))
    vo(nc.vector.tensor_scalar(r[4], vcol(m, "rg_bx", 0, 2 * KR), 0.5, None, ALU.mult))


class Stats:

    def __init__(self, nc, m, tag, ntok, diag, acc=None):
        self.nc, self.m, self.ntok, self.diag = nc, m, ntok, diag
        self.acc = m.acc if acc is None else acc
        self.nt = ntok // P
        self.sum_done, self.root_ready, self.recip_ready, self.diag_ready, self.rstd_ready = [
            m.sem(f"{tag}_{n}") for n in ("sum_done", "root_ready", "recip_ready", "diag_ready", "rstd_ready")]
        self.rstd = m.ps[:, SLOT:SLOT + ntok]

    def pe(self, pe):
        nc, m = self.nc, self.m
        for i in range(self.nt):
            nc.tensor.matmul(m.ps[:, MISC + i:MISC + i + 1], self.acc[:, i * P:(i + 1) * P], m.ones[:, 0:1], start=True, stop=False)
            ins = nc.tensor.matmul(m.ps[:, MISC + i:MISC + i + 1], m.sq[:, (KD - 1) % 2, i * P:(i + 1) * P], m.ones[:, 0:1], start=False, stop=True)
        ins.then_inc(self.sum_done, 1)
        pe.wait_ge(self.diag_ready, 1)
        for c, n in chunks(self.ntok):
            ins = nc.tensor.matmul(m.ps[:, SLOT + c:SLOT + c + n], m.ones[:, :], self.diag[:, c // P:(c + n) // P, :], start=True, stop=True)
        ins.then_inc(self.rstd_ready, 1)

    def act(self, act):
        act.wait_ge(self.sum_done, 1)
        self.nc.scalar.activation(self.m.root[:, 0:self.nt], self.m.ps[:, MISC:MISC + self.nt], ACT.Sqrt,
                                  bias=self.m.eps[:, :], scale=1.0 / D).then_inc(self.root_ready, 1)

    def dve(self, dve):
        nc, m, nt = self.nc, self.m, self.nt
        dve.wait_ge(self.root_ready, 1)
        nc.vector.reciprocal(m.root[:, 0:nt], m.root[:, 0:nt]).then_inc(self.recip_ready, 1)
        dve.wait_ge(self.recip_ready, 1)
        nc.vector.tensor_tensor(self.diag[:, 0:nt, :], m.ident[:, :].unsqueeze(1).to_broadcast([P, nt, P]),
                                m.root[:, 0:nt].unsqueeze(2).to_broadcast([P, nt, P]), ALU.mult).then_inc(self.diag_ready, 1)
        dve.wait_ge(self.rstd_ready, 1)


class Norm:

    def __init__(self, nc, m, l, which, ntok, ztmp, diag, acc=None):
        tag = f"n{l}{which}"
        self.nc, self.m, self.l, self.which, self.ntok, self.ztmp = nc, m, l, which, ntok, ztmp
        self.stats = Stats(nc, m, tag, ntok, diag, acc)
        self.scaled, self.high, self.low = [m.sem(f"{tag}_{n}") for n in ("scaled", "high", "low")]
        self.shift = 3 * which * KD
        self.ns = len(segs(ntok))

    def wait_z(self, pe, k):
        pe.wait_ge(self.low, self.ns * (k + 1))

    def act(self, act):
        nc, m = self.nc, self.m
        self.stats.act(act)
        for k in range(KD):
            act.wait_ge(self.scaled, k + 1)
            for s, (a, b) in enumerate(segs(self.ntok)):
                nc.scalar.activation(m.zH[:, k, a:b], self.ztmp[:, k % 2, a:b], ACT.Identity,
                                     bias=m.mod[:, self.l, s, self.shift + k:self.shift + k + 1]).then_inc(self.high, 1)

    def dve(self, dve):
        nc, m, ns = self.nc, self.m, self.ns
        self.stats.dve(dve)
        for k in range(KD + 1):
            if k < KD:
                if k >= 2:
                    dve.wait_ge(self.low, ns * (k - 1))
                for s, (a, b) in enumerate(segs(self.ntok)):
                    ins = nc.vector.scalar_tensor_tensor(out=self.ztmp[:, k % 2, a:b], in0=m.res[:, k, a:b],
                                                         scalar=m.gain[:, self.l, self.which, s, k:k + 1], in1=self.stats.rstd[:, a:b],
                                                         op0=ALU.mult, op1=ALU.mult)
                    if s == ns - 1:
                        ins.then_inc(self.scaled, 1)
            if k > 0:
                j = k - 1
                dve.wait_ge(self.high, ns * (j + 1))
                for s, (a, b) in enumerate(segs(self.ntok)):
                    nc.vector.scalar_tensor_tensor(out=m.zL[:, j, a:b], in0=self.ztmp[:, j % 2, a:b],
                                                   scalar=m.mod[:, self.l, s, self.shift + j:self.shift + j + 1],
                                                   in1=m.zH[:, j, a:b].bitcast(F32), op0=ALU.add, op1=ALU.subtract).then_inc(self.low, 1)


class Squares:

    def __init__(self, nc, m, tag, ntok):
        self.nc, self.m, self.ntok = nc, m, ntok
        self.sq_ready, self.acc_done = m.sem(tag + "sq_ready"), m.sem(tag + "acc_done")

    def square(self, act, tile, s):
        act.wait_ge(self.acc_done, tile + 2)
        src = self.m.res[:, ds(tile, 1), 0:self.ntok].rearrange("p a t -> p (a t)")
        self.nc.scalar.activation(self.m.sq[:, s, 0:self.ntok], src, ACT.Square).then_inc(self.sq_ready, 1)

    def clear(self, gp):
        prime(gp, (self.acc_done, 2))
        self.nc.gpsimd.memset(self.m.acc[:, :], 0.0).then_inc(self.acc_done, 1)

    def add(self, gp, tile, s):
        gp.wait_ge(self.sq_ready, tile + 1)
        gp.wait_ge(self.acc_done, tile + 3)
        acc = self.m.acc[:, 0:self.ntok]
        self.nc.gpsimd.tensor_tensor(acc, acc, self.m.sq[:, s, 0:self.ntok], ALU.add).then_inc(self.acc_done, 1)


def product(nc, ps, slot, ntok, wH, wL, rH, rL, K, wait_input=None):
    last = None
    for k in range(K):
        if wait_input is not None:
            wait_input(k)
        for i, (w, r) in enumerate(((wH, rH), (wH, rL), (wL, rH))):
            for c, n in chunks(ntok):
                last = nc.tensor.matmul(ps[:, slot * SLOT + c:slot * SLOT + c + n], w(k), r(k)[:, c:c + n],
                                        start=(k == 0 and i == 0), stop=(k == K - 1 and i == 2))
    return last


def modulation_tile(nc, m, at, q, slot):
    for k in range(KD):
        last = nc.tensor.matmul(m.ps[:, at + 2 * q:at + 2 * q + 2], m.modw[:, slot, k, :], m.ccol[:, k, :], start=(k == 0), stop=(k == KD - 1))
    return last


def taps(nc, dve, order, dst, src, ws, ntok):
    for shift, w in ws:
        for a, b in segs(ntok):
            lo, hi = max(a, a - shift), min(b, b - shift)
            order(nc.vector.scalar_tensor_tensor(out=dst[:, lo:hi], in0=src[:, lo + shift:hi + shift], scalar=w, in1=dst[:, lo:hi],
                                                 op0=ALU.mult, op1=ALU.add))


def rglru(nc, m):
    t, sem, ps = m.t, m.sem, m.ps
    raw_in = [sem(f"rg_raw_in{i}") for i in range(3)]
    norm1 = Norm(nc, m, 0, 0, TOK, m.sq, m.diag, m.acc0)
    w_high, w_ready = sem("rg_w_high"), sem("rg_w_ready")
    unit_done, psum_free = sem("rg_unit_done"), [sem("rg_psum_free0"), sem("rg_psum_free1")]
    gw_in = sem("rg_gw_in")
    x_mid, x_ready, taps_order = sem("rg_x_mid"), sem("rg_x_ready"), sem("rg_taps_order")
    g_ready, tr_ready, ti_ready, a_ready, t2_ready, sq_ready = [sem("rg_" + n) for n in ("g_ready", "tr_ready", "ti_ready", "a_ready", "t2_ready", "sq_ready")]
    scans, dir_order, y_ready, y_out = sem("rg_scans"), sem("rg_dir_order"), sem("rg_y_ready"), sem("rg_y_out")
    mod_in, mod_used, mod_copied = [sem("rg_mod_in0"), sem("rg_mod_in1")], sem("rg_mod_used"), sem("rg_mod_copied")
    y_stored = sem("rg_y_stored")

    seq = [("x", 0)]
    for j in range(HALF):
        if j + 1 < HALF:
            seq.append(("x", j + 1))
        seq.append(("g", j))
        seq += [("r0", j), ("i0", j), ("r1", j), ("i1", j)]
    U = len(seq)
    assert U % 2 == 0
    blocks = [(k, j) for k, j in seq if k in "xg"]
    NB = len(blocks)
    block_unit = [u for u, (k, j) in enumerate(seq) if k in "xg"]
    UNITS_AFTER = U - 1 - block_unit[-1]

    def units(n):
        return primed(n, UNITS_AFTER + 1)

    per_slot = [len(range(s, NB, 3)) for s in range(3)]
    GR = len(RECTS) * 2

    def mods_after(kind, j):
        if j == HALF - 1:
            return {"i0": 1, "r1": 1, "i1": 2}.get(kind, 0)
        return int(kind in ("i0", "i1"))

    MH = sum(mods_after(kind, j) for kind, j in seq)
    MOD_HEAD = N_MOD - 2 * KD - 2 * MH
    MOD_FIRST = 2 * KD + MOD_HEAD
    assert MOD_HEAD > 0 and MOD_HEAD % 2 == 0 and MH % 2 == 0
    w_in = t["rg_w_in"][0].rearrange("(k p) n -> p k n", p=P)
    mod_w = t["mod_w"][0].rearrange("(k p) n -> p k n", p=P)
    gate_w = {"r": t["rg_wa"][0], "i": t["rg_wx"][0]}
    kinds = ["r0", "i0", "r1", "i1"]
    n_taps = 6

    with nc.Block() as block:
        @block.sync
        def _(sp):
            with sp.Fori(0, 2) as h:
                h4 = sp.snap(4 * h)
                for b, (kind, j) in enumerate(blocks):
                    if b == 3:
                        sp.wait_ge(unit_done, units(U * h))
                        for p, blk, r, rb, nr, c, cb, ncol in RECTS:
                            for g, gk in enumerate("ri"):
                                srcw = gate_w[gk][:, ds(h4 + blk, 1), rb:rb + nr, cb:cb + ncol].rearrange("d a r c -> (a r) d c")
                                sp.dma_start(m.gW[r:r + nr, g::2, p, c:c + ncol], srcw).then_inc(gw_in, 16)
                    if b == 0 or b >= 3:
                        sp.wait_ge(w_ready, primed(NB * h + b - 2 if b >= 3 else NB * h))
                    col = (0 if kind == "g" else D_RNN) + P * j
                    sp.dma_start(m.wraw[:, b % 3, :].rearrange("p (k n) -> p k n", k=KD), w_in[:, :, ds(HALF * P * h + col, P)]).then_inc(raw_in[b % 3], 16)

        @block.gpsimd
        def _(gp):
            prime(gp, (y_stored, 1))
            gp.wait_ge(norm1.stats.sum_done, 1)
            for q in range(MOD_HEAD):
                if q >= 2:
                    gp.wait_ge(mod_used, primed(q - 1))
                gp.dma_start(m.modw[:, q % 2, :, :], mod_w[:, :, (2 * KD + q) * P:(2 * KD + q + 1) * P]).then_inc(mod_in[q % 2], 16)
            with gp.Fori(0, 2) as h:
                q = 0
                for j in range(HALF):
                    for _ in range(sum(mods_after(kind, i) for kind, i in seq if i == j and kind not in "xg")):
                        gp.wait_ge(mod_used, primed(MH * h + (MOD_HEAD + q - 1)))
                        gp.dma_start(m.modw[:, q % 2, :, :], mod_w[:, :, ds(MH * P * h + (MOD_FIRST + q) * P, P)]).then_inc(mod_in[q % 2], 16)
                        q += 1
                    gp.wait_ge(y_ready, primed(HALF * h + j + 1))
                    gp.dma_start(m.yT[ds(HALF * h + j, 1)].rearrange("a p t -> (a p) t"), m.TR[:, 0, :]).then_inc(y_out, 16)
                    gp.wait_ge(y_out, 16 * HALF * h + 16 * (j + 1))
                    gp.nop().then_inc(y_stored, 1)

        @block.tensor
        def _(pe):
            prime(pe, (unit_done, UNITS_AFTER + 1), (mod_used, 1))
            norm1.stats.pe(pe)
            for q in range(MOD_HEAD):
                pe.wait_ge(mod_in[q % 2], 16 * (q // 2 + 1))
                modulation_tile(nc, m, MISC + BANK, q, q % 2).then_inc(mod_used, 1)
            with pe.Fori(0, 2) as h:
                b = q = 0
                for u, (kind, j) in enumerate(seq):
                    s = u % 2
                    pe.wait_ge(psum_free[s], primed((U // 2) * h + u // 2))
                    if kind in "xg":
                        pe.wait_ge(w_ready, primed(NB * h + b + 1))
                        wH = m.wH[:, b % 3, :]
                        wL = m.wL[:, b % 3, :]
                        ins = product(nc, ps, s, TOK, lambda k: wH[:, k * P:(k + 1) * P], lambda k: wL[:, k * P:(k + 1) * P],
                                      lambda k: m.zH[:, k, :], lambda k: m.zL[:, k, :], KD,
                                      (lambda k: norm1.wait_z(pe, k)) if u == 0 else None)
                        ins.then_inc(unit_done, 1)
                        b += 1
                    else:
                        pe.wait_ge(x_ready, HALF * h + min(j + 2, HALF))
                        if j == 0 and kind == "r0":
                            pe.wait_ge(gw_in, 16 * GR * h + 16 * GR)
                        steps = [(p, kt) for p, (mt, kt) in enumerate(PAIRS) if mt == j]
                        for n, (p, kt) in enumerate(steps):
                            for c, w in chunks(TOK):
                                ins = nc.tensor.matmul(ps[:, s * SLOT + c:s * SLOT + c + w], m.gW[:, kinds.index(kind), p, :],
                                                       m.x[:, kt, c:c + w], start=(n == 0), stop=(n == len(steps) - 1))
                        ins.then_inc(unit_done, 1)
                        for _ in range(mods_after(kind, j)):
                            pe.wait_ge(mod_in[q % 2], (16 * MH // 2) * h + 16 * ((MOD_HEAD + q) // 2 + 1))
                            if q == 0:
                                pe.wait_ge(mod_copied, primed(h + 1))
                            modulation_tile(nc, m, MISC + BANK, q, q % 2).then_inc(mod_used, 1)
                            q += 1

        @block.scalar
        def _(act):
            def split(h, b):
                act.wait_ge(raw_in[b % 3], 16 * per_slot[b % 3] * h + 16 * (b // 3 + 1))
                act.wait_ge(unit_done, units(U * h + block_unit[b - 3] + 1) if b >= 3 else units(U * h - UNITS_AFTER))
                nc.scalar.activation(m.wH[:, b % 3, :], m.wraw[:, b % 3, :], ACT.Copy).then_inc(w_high, 1)

            norm1.act(act)
            with act.Fori(0, 2) as h:
                for b in range(3):
                    split(h, b)
                b = 3
                for u, (kind, j) in enumerate(seq):
                    src = ps[:, (u % 2) * SLOT:(u % 2) * SLOT + TOK]
                    act.wait_ge(unit_done, units(U * h + u + 1))
                    if kind == "x":
                        act.wait_ge(y_ready, primed(HALF * h))
                        nc.scalar.activation(m.x[:, j, :], src, ACT.Identity, scale=colreg(m, "rg_conv_w", 2 * KR + j, HALF * h),
                                             bias=colreg(m, "rg_conv_b", j, HALF * h)).then_inc(x_mid, 1)
                    elif kind == "g":
                        act.wait_ge(y_ready, primed(HALF * h + j))
                        nc.scalar.activation(m.GG[:, :], src, ACT.Gelu_apprx_tanh).then_inc(g_ready, 1)
                        act.wait_ge(g_ready, HALF * h + j + 1)
                        act.nop().then_inc(psum_free[u % 2], 1)
                    else:
                        d = int(kind[1])
                        n = 2 * j + d
                        if kind[0] == "r":
                            if d == 0:
                                act.wait_ge(y_stored, primed(HALF * h + j))
                            else:
                                act.wait_ge(y_ready, primed(HALF * h + j))
                            nc.scalar.activation(m.TR[:, d, :], src, ACT.Tanh, scale=0.5,
                                                 bias=lrucol(m, 3, KR * d + j, HALF * h)).then_inc(tr_ready, 1)
                            act.wait_ge(tr_ready, 2 * HALF * h + n + 1)
                            act.nop().then_inc(psum_free[u % 2], 1)
                        else:
                            act.wait_ge(scans, primed(2 * HALF * h + n))
                            nc.scalar.activation(m.TI[:, :], src, ACT.Tanh, scale=0.5,
                                                 bias=lrucol(m, 4, KR * d + j, HALF * h)).then_inc(ti_ready, 1)
                            act.wait_ge(ti_ready, 2 * HALF * h + n + 1)
                            act.nop().then_inc(psum_free[u % 2], 1)
                            nc.scalar.activation(m.A[:, :], m.TR[:, d, :], ACT.Exp, scale=lrucol(m, 2, KR * d + j, HALF * h),
                                                 bias=lrucol(m, 2, KR * d + j, HALF * h)).then_inc(a_ready, 1)
                            act.wait_ge(a_ready, 2 * HALF * h + n + 1)
                            nc.scalar.activation(m.TR[:, d, :], m.TR[:, d, :], ACT.Tanh, scale=lrucol(m, 0, KR * d + j, HALF * h),
                                                 bias=lrucol(m, 0, KR * d + j, HALF * h)).then_inc(t2_ready, 1)
                            act.wait_ge(t2_ready, 2 * HALF * h + n + 1)
                            nc.scalar.activation(m.TR[:, d, :], m.TR[:, d, :], ACT.Sqrt).then_inc(sq_ready, 1)
                    if kind in "xg" and b < NB:
                        split(h, b)
                        b += 1

        @block.vector
        def _(dve):
            prime(dve, (w_ready, 1), (y_ready, 1), (scans, 1), (psum_free[0], 1), (psum_free[1], 1), (mod_copied, 1))

            def split(h, b):
                dve.wait_ge(w_high, NB * h + b + 1)
                nc.vector.tensor_tensor(m.wL[:, b % 3, :], m.wraw[:, b % 3, :], m.wH[:, b % 3, :].bitcast(F32), ALU.subtract).then_inc(w_ready, 1)

            def copy_modulation(used, tile, n):
                dve.wait_ge(mod_used, primed(used))
                for s in range(2):
                    ins = nc.vector.tensor_tensor(m.mod[:, 0, s, ds(tile, n)], ps[:, MISC + BANK + s:MISC + BANK + 2 * n:2],
                                                  m.vec[:, ds(tile + VEC_AT["mod_b"], n)], ALU.add)
                ins.then_inc(mod_copied, 1)

            norm1.dve(dve)
            copy_modulation(MOD_HEAD, 2 * KD, MOD_HEAD)
            with dve.Fori(0, 2) as h:
                for b in range(3):
                    split(h, b)
                b = 3
                to = Order(dve, taps_order, n_taps * HALF * h)
                do = Order(dve, dir_order, (2 * 3 + 1 + 1) * HALF * h)
                for u, (kind, j) in enumerate(seq):
                    s = u % 2
                    src = ps[:, s * SLOT:s * SLOT + TOK]
                    if kind == "x":
                        dve.wait_ge(x_mid, HALF * h + j + 1)
                        taps(nc, dve, to, m.x[:, j, :], src, [(-2, colreg(m, "rg_conv_w", j, HALF * h)),
                                                              (-1, colreg(m, "rg_conv_w", KR + j, HALF * h)),
                                                              (1, colreg(m, "rg_conv_w", 3 * KR + j, HALF * h))], TOK)
                        dve.nop().then_inc(x_ready, 1)
                        dve.nop().then_inc(psum_free[s], 1)
                    if kind in ("i0", "i1"):
                        d = int(kind[1])
                        n = 2 * j + d
                        dve.wait_ge(ti_ready, 2 * HALF * h + n + 1)
                        do(nc.vector.scalar_tensor_tensor(out=m.TI[:, :], in0=m.TI[:, :], scalar=1.0, in1=m.x[:, j, :], op0=ALU.add, op1=ALU.mult))
                        dve.wait_ge(sq_ready, 2 * HALF * h + n + 1)
                        do(nc.vector.scalar_tensor_tensor(out=m.TR[:, d, :], in0=m.A[:, :], scalar=1.0, in1=m.TR[:, d, :], op0=ALU.add, op1=ALU.mult))
                        do(nc.vector.tensor_tensor(m.TI[:, :], m.TI[:, :], m.TR[:, d, :], ALU.mult))
                        if d == 0:
                            do(nc.vector.tensor_tensor_scan(out=m.TR[:, 0, SEQ:TOK], data0=m.A[:, SEQ:TOK], data1=m.TI[:, SEQ:TOK],
                                                            initial=0.0, op0=ALU.mult, op1=ALU.add))
                            nc.vector.tensor_tensor_scan(out=m.TR[:, 0, 0:SEQ], data0=m.A[:, 0:SEQ], data1=m.TI[:, 0:SEQ],
                                                         initial=m.TR[:, 0, TOK - 1:TOK], op0=ALU.mult, op1=ALU.add).then_inc(scans, 1)
                        else:
                            nc.vector.tensor_tensor_scan(out=m.TR[:, 1, ::-1], data0=m.A[:, ::-1], data1=m.TI[:, ::-1],
                                                         initial=0.0, op0=ALU.mult, op1=ALU.add).then_inc(scans, 1)
                        dve.wait_ge(scans, primed(2 * HALF * h + n + 1))
                        if d == 1:
                            do(nc.vector.tensor_tensor(m.TR[:, 0, :], m.TR[:, 0, :], m.TR[:, 1, :], ALU.add))
                            dve.wait_ge(g_ready, HALF * h + j + 1)
                            nc.vector.tensor_tensor(m.TR[:, 0, :], m.TR[:, 0, :], m.GG[:, :], ALU.mult).then_inc(y_ready, 1)
                    if kind in "xg" and b < NB:
                        split(h, b)
                        b += 1
                copy_modulation(MH * h + (MOD_HEAD + MH), MH * h + MOD_FIRST, MH)
            dve.wait_ge(mod_copied, primed(3))
            for s in range(2):
                nc.vector.scalar_tensor_tensor(out=m.gain[:, 0, 1, s, :], in0=m.mod[:, 0, s, 4 * KD:5 * KD], scalar=1.0,
                                               in1=vcol(m, "norm2_g", 0, KD), op0=ALU.add, op1=ALU.mult)
                nc.vector.tensor_scalar(m.gate[:, s, :], m.mod[:, 0, s, 2 * KD:3 * KD], 0.5, None, ALU.mult)


def colreg(m, name, i, reg):
    return m.vec[:, ds(reg + (VEC_AT[name] + i), 1)]


def lrucol(m, row, i, reg):
    return m.lru[:, row, ds(reg + i, 1)]


def project(nc, m, l, w, K, ntok):
    sem, ps = m.sem, m.ps
    tag = f"p{l}_"
    y_in = [sem(tag + f"y_in{k}") for k in range(K)]
    y_high, y_ready = sem(tag + "y_high"), sem(tag + "y_ready")
    w_raw = [sem(tag + "w_raw0"), sem(tag + "w_raw1")]
    w_high, w_ready, unit_done = sem(tag + "w_high"), sem(tag + "w_ready"), sem(tag + "unit_done")
    psum_free = [sem(tag + "psum_free0"), sem(tag + "psum_free1")]
    res_in = [sem(tag + f"res_in{k}") for k in range(KD)]
    wv = w.rearrange("(k p) n -> p k n", p=P)
    squares = Squares(nc, m, tag, ntok)
    bias_made = sem(tag + "bias_made")

    def yH(k):
        return m.zH[:, k, :] if k < KD else m.yH[:, k - KD, :]

    def yL(k):
        return m.zL[:, k, :] if k < KD else m.yL[:, k - KD, :]

    def yraw(k):
        return (m.zLraw[:, k, :] if k < KD else m.yLraw[:, k - KD, :])[:, 0:ntok]

    def unit(pe, s, first, wait_ready, wait_free):
        pe.wait_ge(w_ready, wait_ready)
        if wait_free is not None:
            pe.wait_ge(psum_free[s], wait_free)
        for k in range(K):
            if first:
                pe.wait_ge(y_ready, k + 1)
            for i, (wt, r) in enumerate(((m.oH, yH(k)), (m.oH, yL(k)), (m.oL, yH(k)))):
                for c, n in chunks(ntok):
                    ins = nc.tensor.matmul(ps[:, s * SLOT + c:s * SLOT + c + n], wt[:, s, k, :], r[:, c:c + n],
                                           start=(k == 0 and i == 0), stop=(k == K - 1 and i == 2))
        ins.then_inc(unit_done, 1)

    with nc.Block() as block:
        @block.sync
        def _(sp):
            sp.dma_start(m.oraw[:, 0, 0:K, :], wv[:, :, 0:P]).then_inc(w_raw[0], 16)
            for k in range(K):
                sp.dma_start(yraw(k), m.yT[k][:, 0:ntok]).then_inc(y_in[k], 16)
                if k == 2:
                    sp.dma_start(m.oraw[:, 1, 0:K, :], wv[:, :, P:2 * P]).then_inc(w_raw[1], 16)
            if l == 0:
                for k in range(KD):
                    sp.dma_start(m.res[:, k, :], m.xT[k]).then_inc(res_in[k], 16)
            with sp.Fori(1, KD // 2) as i:
                for s in range(2):
                    sp.wait_ge(w_ready, 2 * i + s - 1)
                    sp.dma_start(m.oraw[:, s, 0:K, :], wv[:, :, ds(2 * P * i + s * P, P)]).then_inc(w_raw[s], 16)

        @block.scalar
        def _(act):
            def first_w_high(s):
                act.wait_ge(w_raw[s], 16)
                nc.scalar.activation(m.oH[:, s, 0:K, :], m.oraw[:, s, 0:K, :], ACT.Copy).then_inc(w_high, 1)

            first_w_high(0)
            for k in range(K):
                if k == 4:
                    first_w_high(1)
                act.wait_ge(y_in[k], 16)
                nc.scalar.activation(yH(k)[:, 0:ntok], yraw(k), ACT.Copy).then_inc(y_high, 1)
            with act.Fori(1, KD // 2) as i:
                for s in range(2):
                    act.wait_ge(w_raw[s], 16 * i + 16)
                    act.wait_ge(unit_done, 2 * i + s - 1)
                    nc.scalar.activation(m.oH[:, s, 0:K, :], m.oraw[:, s, 0:K, :], ACT.Copy).then_inc(w_high, 1)
                    act.wait_ge(psum_free[s], i)
                    squares.square(act, 2 * i + s - 2, s)
            for s in range(2):
                act.wait_ge(psum_free[s], KD // 2)
                squares.square(act, KD - 2 + s, s)

        @block.gpsimd
        def _(gp):
            squares.clear(gp)
            if l == 0:
                with gp.Fori(0, GW) as q:
                    gp.dma_start(m.biasT[:, ds(q, 1), :, :].rearrange("h a r c -> h (a r) c"), m.rpbT[:, :, ds(GW - 1 - q, GW)]).then_inc(bias_made, 16)
            with gp.Fori(0, KD // 2 - 1) as i:
                for s in range(2):
                    squares.add(gp, 2 * i + s, s)
            squares.add(gp, KD - 2, 0)
            if l == 0:
                gp.wait_ge(bias_made, 16 * GW)

        @block.tensor
        def _(pe):
            for s in range(2):
                unit(pe, s, s == 0, s + 1, None)
            with pe.Fori(1, KD // 2) as i:
                for s in range(2):
                    unit(pe, s, False, 2 * i + s + 1, i)

        @block.vector
        def _(dve):
            def w_low(s, ready):
                dve.wait_ge(w_high, ready)
                nc.vector.tensor_tensor(m.oL[:, s, 0:K, :], m.oraw[:, s, 0:K, :], m.oH[:, s, 0:K, :].bitcast(F32), ALU.subtract).then_inc(w_ready, 1)

            def add(s, tile, done):
                dve.wait_ge(unit_done, done)
                mt = ds(tile, 1)
                for g, (a, b) in enumerate(segs(ntok)):
                    gt = m.gate[:, g, mt] if l == 0 else m.mod[:, l, g, ds(tile + 2 * KD, 1)]
                    r = m.res[:, mt, a:b].rearrange("p a t -> p (a t)")
                    ins = nc.vector.scalar_tensor_tensor(out=r, in0=ps[:, s * SLOT + a:s * SLOT + b], scalar=gt, in1=r, op0=ALU.mult, op1=ALU.add)
                ins.then_inc(psum_free[s], 1)

            w_low(0, 1)
            for k in range(K):
                if k == 4:
                    w_low(1, 2)
                dve.wait_ge(y_high, k + 1)
                nc.vector.tensor_tensor(yL(k)[:, 0:ntok], yraw(k), yH(k)[:, 0:ntok].bitcast(F32), ALU.subtract).then_inc(y_ready, 1)
            if l == 0:
                for k in range(KD):
                    dve.wait_ge(res_in[k], 16)
            with dve.Fori(0, KD // 2 - 1) as i:
                for s in range(2):
                    add(s, 2 * i + s, 2 * i + s + 1)
                    w_low(s, 2 * i + s + 3)
            for s in range(2):
                add(s, KD - 2 + s, KD - 1 + s)


def ffn(nc, m, l, ntok):
    t, sem, ps = m.t, m.sem, m.ps
    tag = f"f{l}_"
    raw_in = [sem(tag + f"raw_in{i}") for i in range(3)]
    w_high, w_ready = sem(tag + "w_high"), sem(tag + "w_ready")
    unit_done, psum_free = sem(tag + "unit_done"), [sem(tag + "psum_free0"), sem(tag + "psum_free1")]
    mid, taps_order, g_conv, v_conv = sem(tag + "mid"), sem(tag + "taps_order"), sem(tag + "g_conv"), sem(tag + "v_conv")
    silu_done, h_full, h_high, h_ready = [sem(tag + n) for n in ("silu_done", "h_full", "h_high", "h_ready")]
    norm2 = Norm(nc, m, l, 1, ntok, m.sq, m.diag)
    squares = Squares(nc, m, tag, ntok)
    mod_in, mod_used, mod_copied = [sem(tag + "mod_in0"), sem(tag + "mod_in1")], sem(tag + "mod_used"), sem(tag + "mod_copied")
    up = t["ffn_w_up"][l].rearrange("(k p) n -> p k n", p=P)
    down = t["ffn_w_down"][l].rearrange("(k p) n -> k p n", p=P)
    mod_w = t["mod_w"][1].rearrange("(k p) n -> p k n", p=P)
    NG = KF // 2
    ns = len(segs(ntok))
    HEAD = [("g", 0), ("v", 0), ("g", 1), ("v", 1)]
    BODY = [("g", 0), ("d", 0), ("v", 0), ("g", 1), ("v", 1)]
    TAIL = [("d", 0)]
    with_mod = l == 0
    MPG = 1 if with_mod else 0
    MOD_HEAD = 2 * KD - (NG - 1) if with_mod else 0
    HEAD_MODS = [2, 0, 1, 1, 1, 1, 0, 0]
    assert not with_mod or sum(HEAD_MODS) == MOD_HEAD

    def program(eng, group):
        group(HEAD, 0, 0, 0, True)
        with eng.Fori(1, NG - 1) as i:
            group(BODY, i, 6 * i - 2, 12 * i - 8, False)
        group(BODY, NG - 1, 6 * (NG - 1) - 2, 12 * (NG - 1) - 8, False)
        group(TAIL, NG, 6 * NG - 2, 12 * NG - 8, False)

    def slot(first, k):
        return (k if first else k + 1) % 3

    def raw_count(first, i, k):
        if first:
            return 16 * (k // 3 + 1)
        s = (k + 1) % 3
        before = 2 if s == 0 else 1
        return 32 * i - 32 + 16 * before + 16 * ((k - (s - 1) % 3) // 3 + 1)

    def block_list(part):
        out = []
        for kind, j in part:
            out += [("d", 0), ("d", 1)] if kind == "d" else [(kind, j)]
        return out

    with nc.Block() as block:
        @block.sync
        def _(sp):
            def group(part, i, b0, u0, first):
                for k, (kind, j) in enumerate(block_list(part)):
                    s = slot(first, k)
                    if not (first and k < 3):
                        sp.wait_ge(w_ready, b0 + k - 2)
                    if kind == "d":
                        src = down[ds(2 * i - 2 + j, 1)].rearrange("a p n -> (a p) n")
                        sp.dma_start(m.wraw[:, s, :], src).then_inc(raw_in[s], 16)
                    else:
                        col = (0 if kind == "g" else D_FF) + P * j
                        sp.dma_start(m.wraw[:, s, :].rearrange("p (k n) -> p k n", k=KD), up[:, :, ds(2 * P * i + col, P)]).then_inc(raw_in[s], 16)
            program(sp, group)

        @block.gpsimd
        def _(gp):
            def modulation_weights():
                def group(part, i, b0, u0, first):
                    if part is TAIL:
                        return
                    if first:
                        for q in range(MOD_HEAD):
                            if q >= 2:
                                gp.wait_ge(mod_used, q - 1)
                            gp.dma_start(m.modw[:, q % 2, :, :], mod_w[:, :, q * P:(q + 1) * P]).then_inc(mod_in[q % 2], 16)
                    elif MPG:
                        gp.wait_ge(mod_used, i + (MOD_HEAD - 1))
                        gp.dma_start(m.modw[:, 0, :, :], mod_w[:, :, ds(P * i + (MOD_HEAD - 1) * P, P)]).then_inc(mod_in[0], 16)
                program(gp, group)

            modulation_weights()
            gp.wait_ge(norm2.stats.sum_done, 1)
            squares.clear(gp)
            for mt in range(KD - 1):
                squares.add(gp, mt, mt % 2)

        @block.tensor
        def _(pe):
            def modulation(i, q, first):
                if first:
                    pe.wait_ge(mod_in[q % 2], 16 * (q // 2 + 1))
                else:
                    pe.wait_ge(mod_in[0], 16 * i + 16 * MOD_HEAD // 2)
                    pe.wait_ge(mod_copied, i)
                modulation_tile(nc, m, MISC + BANK, q, q % 2).then_inc(mod_used, 1)

            def next_input(k):
                for q in range(sum(HEAD_MODS[0:k]), sum(HEAD_MODS[0:k + 1]) if with_mod else 0):
                    modulation(0, q, True)
                norm2.wait_z(pe, k)

            def group(part, i, b0, u0, first):
                k = u = 0
                for kind, j in part:
                    if kind != "d":
                        s = u % 2
                        if not (first and u < 2):
                            pe.wait_ge(psum_free[s], free(first, i, u))
                        pe.wait_ge(w_ready, b0 + k + 1)
                        wH, wL = m.wH[:, slot(first, k), :], m.wL[:, slot(first, k), :]
                        product(nc, ps, s, ntok, lambda n: wH[:, n * P:(n + 1) * P], lambda n: wL[:, n * P:(n + 1) * P],
                                lambda n: m.zH[:, n, :], lambda n: m.zL[:, n, :], KD,
                                next_input if first and u == 0 else None).then_inc(unit_done, 1)
                        u += 1
                        k += 1
                    else:
                        pe.wait_ge(w_ready, b0 + k + 2)
                        pe.wait_ge(h_ready, 2 * i)
                        for mt in range(KD):
                            s = u % 2
                            pe.wait_ge(psum_free[s], free(first, i, u))
                            product(nc, ps, s, ntok, lambda n: m.wH[:, slot(first, k + n), mt * P:(mt + 1) * P],
                                    lambda n: m.wL[:, slot(first, k + n), mt * P:(mt + 1) * P],
                                    lambda n: m.hH[:, n, :], lambda n: m.hL[:, n, :], 2).then_inc(unit_done, 1)
                            if MPG and part is BODY and mt == 0:
                                modulation(i, 0, False)
                            u += 1
                        k += 2
            def free(first, i, u):
                return u // 2 if first else 6 * i + (u // 2 - 4)
            norm2.stats.pe(pe)
            program(pe, group)

        @block.scalar
        def _(act):
            def split(first, i, u0, k, n=1):
                for k in range(k, k + n):
                    s = slot(first, k)
                    act.wait_ge(raw_in[s], raw_count(first, i, k))
                    if not (first and k < 3):
                        act.wait_ge(unit_done, u0 + (k - 2 if first else [1, 9, 9, 10, 11, 12][k - 3]))
                    nc.scalar.activation(m.wH[:, s, :], m.wraw[:, s, :], ACT.Copy).then_inc(w_high, 1)

            def group(part, i, b0, u0, first):
                if first:
                    split(True, 0, 0, 0, 2)
                    norm2.act(act)
                    split(True, 0, 0, 2)
                k = u = 0
                for kind, j in part:
                    if kind != "d":
                        src = ps[:, (u % 2) * SLOT:(u % 2) * SLOT + ntok]
                        act.wait_ge(unit_done, u0 + u + 1)
                        dst = m.G if kind == "g" else m.V
                        act.wait_ge(h_ready, 2 * i + j)
                        col = 2 * i + ((0 if kind == "g" else KF) + j)
                        nc.scalar.activation(dst[:, 0:ntok], src, ACT.Identity, scale=fcol(m, l, 1, col), bias=fcol(m, l, 3, col)).then_inc(mid, 1)
                        after(first, i, u0, k + 3, part)
                        if kind == "g":
                            act.wait_ge(g_conv, 2 * i + j + 1)
                            nc.scalar.activation(m.G[:, 0:ntok], m.G[:, 0:ntok], ACT.Silu).then_inc(silu_done, 1)
                        else:
                            act.wait_ge(h_full, 2 * i + j + 1)
                            nc.scalar.activation(m.hH[:, j, 0:ntok], m.V[:, 0:ntok], ACT.Copy).then_inc(h_high, 1)
                        u += 1
                        k += 1
                    elif part is BODY:
                        after(first, i, u0, k + 3, part)
                        after(first, i, u0, k + 4, part)
                        u += 8
                        k += 2

            def after(first, i, u0, k, part):
                if isinstance(i, int) and i == NG - 1 and k >= 8:
                    return
                split(first, i, u0, k)
            program(act, group)
            act.wait_ge(h_ready, KF)
            for mt in range(KD):
                act.wait_ge(psum_free[mt % 2], 6 * NG + (mt // 2 - 3))
                squares.square(act, mt, mt % 2)

        @block.vector
        def _(dve):
            def split(first, i, b0, k, n=1):
                for k in range(k, k + n):
                    s = slot(first, k)
                    dve.wait_ge(w_high, b0 + k + 1)
                    nc.vector.tensor_tensor(m.wL[:, s, :], m.wraw[:, s, :], m.wH[:, s, :].bitcast(F32), ALU.subtract).then_inc(w_ready, 1)

            def after(first, i, b0, k):
                if isinstance(i, int) and i == NG - 1 and k >= 8:
                    return
                split(first, i, b0, k)

            def group(part, i, b0, u0, first):
                if first:
                    split(True, 0, 0, 0, 2)
                    norm2.dve(dve)
                    split(True, 0, 0, 2)
                k = u = 0
                order = Order(dve, taps_order, 4 * (2 * ns) * i)
                for kind, j in part:
                    s = u % 2
                    if kind != "d":
                        src = ps[:, s * SLOT:s * SLOT + ntok]
                        dst = (m.G if kind == "g" else m.V)[:, 0:ntok]
                        dve.wait_ge(mid, u_mid(first, i, part, kind, j))
                        col = 2 * i + ((0 if kind == "g" else KF) + j)
                        taps(nc, dve, order, dst, src, [(-1, fcol(m, l, 0, col)), (1, fcol(m, l, 2, col))], ntok)
                        dve.nop().then_inc(psum_free[s], 1)
                        dve.nop().then_inc(g_conv if kind == "g" else v_conv, 1)
                        if kind == "v":
                            dve.wait_ge(silu_done, 2 * i + j + 1)
                            nc.vector.tensor_tensor(dst, dst, m.G[:, 0:ntok], ALU.mult).then_inc(h_full, 1)
                        after(first, i, b0, k + 3)
                        if kind == "v":
                            dve.wait_ge(h_high, 2 * i + j + 1)
                            nc.vector.tensor_tensor(m.hL[:, j, 0:ntok], dst, m.hH[:, j, 0:ntok].bitcast(F32), ALU.subtract).then_inc(h_ready, 1)
                        u += 1
                        k += 1
                    else:
                        for mt in range(KD):
                            s = u % 2
                            dve.wait_ge(unit_done, u0 + u + 1)
                            if not (isinstance(i, int) and i < 2):
                                dve.wait_ge(psum_free[s], 6 * i + (u // 2 - 4))
                            for g, (a, b) in enumerate(segs(ntok)):
                                ins = nc.vector.scalar_tensor_tensor(out=m.res[:, mt, a:b], in0=ps[:, s * SLOT + a:s * SLOT + b],
                                                                     scalar=m.mod[:, l, g, 5 * KD + mt:5 * KD + mt + 1], in1=m.res[:, mt, a:b],
                                                                     op0=ALU.mult, op1=ALU.add)
                            ins.then_inc(psum_free[s], 1)
                            u += 1
                        if part is BODY:
                            after(first, i, b0, k + 3)
                            after(first, i, b0, k + 4)
                        k += 2
                if with_mod and part is not TAIL:
                    n = MOD_HEAD if first else MPG
                    dve.wait_ge(mod_used, n if first else MPG * i + MOD_HEAD)
                    at = 0 if first else MPG * i + (MOD_HEAD - MPG)
                    for g in range(2):
                        ins = nc.vector.tensor_tensor(m.mod[:, 1, g, ds(at, n)], ps[:, MISC + BANK + g:MISC + BANK + 2 * n:2],
                                                      m.vec[:, ds(at + (VEC_AT["mod_b"] + N_MOD), n)], ALU.add)
                    ins.then_inc(mod_copied, 1)

            def u_mid(first, i, part, kind, j):
                return 4 * i + {("g", 0): 1, ("v", 0): 2, ("g", 1): 3, ("v", 1): 4}[(kind, j)]
            program(dve, group)
            if l == 0:
                dve.wait_ge(mod_copied, NG)
                for g in range(2):
                    nc.vector.scalar_tensor_tensor(out=m.gain[:, 1, 0, g, :], in0=m.mod[:, 1, g, KD:2 * KD], scalar=1.0,
                                                   in1=vcol(m, "norm1_g", KD, KD), op0=ALU.add, op1=ALU.mult)


def fcol(m, l, row, col):
    at = VEC_AT["ffn_conv_b"] + l * 2 * KF if row == 3 else VEC_AT["ffn_conv_w"] + (l * 3 + row) * 2 * KF
    return m.vec[:, ds(col + at, 1)]


def attention(nc, m):
    t, sem, ps = m.t, m.sem, m.ps
    raw_in = [sem(f"na_raw_in{i}") for i in range(2)]
    w_high, w_ready = sem("na_w_high"), sem("na_w_ready")
    qkv_done, q_zero, q_ready, vT_ready, v_T = [sem("na_" + n) for n in ("qkv_done", "q_zero", "q_ready", "vT_ready", "v_T")]
    k_act, k_dve, v_act, v_dve = [sem("na_" + n) for n in ("k_act", "k_dve", "v_act", "v_dve")]
    ctx_copied = sem("na_ctx_copied")
    bias_in, bias_ready = sem("na_bias_in"), sem("na_bias_ready")
    s_done, s_biased, negmax, exp_done, recip, p_ready = [sem("na_" + n) for n in ("s_done", "s_biased", "negmax", "exp_done", "recip", "p_ready")]
    t_done, pT_ready, o_done, o_ready, o_out = [sem("na_" + n) for n in ("t_done", "pT_ready", "o_done", "o_ready", "o_out")]
    o_stored = sem("na_o_stored")
    NP = KD
    w_in = t["na_w_in"][0].rearrange("(k p) n -> p k n", p=P)
    norm1 = Norm(nc, m, 1, 0, TOK, m.na_ztmp, m.na_diag)
    mod_in, mod_used, mod_copied = sem("na_mod_in"), sem("na_mod_used"), sem("na_mod_copied")
    mod_w = t["mod_w"][1].rearrange("(k p) n -> p k n", p=P)
    MOD_FIRST = 2 * KD
    MPP = (N_MOD - MOD_FIRST) // NP
    MOD_ROWS = [3, 8]
    assert len(MOD_ROWS) + 2 == MPP
    TAIL_MODS = SLOT + BANK
    geo = []
    for r in range(ROWS):
        rs = min(max(r - NA_KR // 2, 0), ROWS - NA_KR)
        geo.append((rs, rs - r + NA_KR - 1))

    def program(eng, group):
        with eng.Fori(0, NP - 1) as i:
            group(i, False)
        group(NP - 1, True)

    def sbank(r):
        return (r % 2) * SLOT

    def obank(r):
        return (r % 2) * SLOT + 2 * BANK

    def S(r):
        return m.S[:, r % 3, :] if r % 3 < 2 else m.S2[:, :]

    COLUMNS = [2 * D, 0, D]
    NV = SEQ // P

    with nc.Block() as block:
        @block.sync
        def _(sp):
            def group(i, last):
                for b in range(3):
                    if b != 1:
                        sp.wait_ge(w_ready, primed(3 * i + (1 if b == 2 else 0)))
                    sp.dma_start(m.wraw[:, b % 2, :].rearrange("p (k n) -> p k n", k=KD), w_in[:, :, ds(P * i + COLUMNS[b], P)]).then_inc(raw_in[b % 2], 16)
                sp.wait_ge(s_biased, primed(ROWS * i))
                sp.dma_start(m.bias[:, :, :], m.biasT[ds(2 * i, 2)].rearrange("h q r c -> (h q) r c")).then_inc(bias_in, 16)
            program(sp, group)

        @block.gpsimd
        def _(gp):
            def bias(i):
                gp.wait_ge(bias_in, 16 * i + 16)
                nc.gpsimd.tensor_tensor(m.bias[:, :, :], m.bias[:, :, :], m.mask[:, :].unsqueeze(1).to_broadcast([P, 15, GW]), ALU.add).then_inc(bias_ready, 1)

            def group(i, last):
                for q in range(MPP):
                    gp.wait_ge(mod_used, primed(MPP * i + q))
                    gp.dma_start(m.modw[:, 1, :, :], mod_w[:, :, ds(MPP * P * i + (MOD_FIRST + q) * P, P)]).then_inc(mod_in, 16)
                    if q == 0:
                        bias(i)
                gp.wait_ge(o_ready, primed(ROWS * i + ROWS))
                gp.dma_start(m.yT[ds(i, 1)].rearrange("a p t -> (a p) t")[:, 0:SEQ], m.oT[:, :]).then_inc(o_out, 16)
                gp.wait_ge(o_out, 16 * i + 16)
                gp.nop().then_inc(o_stored, 1)
            prime(gp, (o_stored, 1))
            gp.wait_ge(norm1.stats.sum_done, 1)
            nc.gpsimd.memset(m.qbd[:, :, :], 0.0).then_inc(q_zero, 1)
            program(gp, group)

        @block.tensor
        def _(pe):
            prime(pe, (qkv_done, 1), (o_done, 1), (mod_used, 1))

            def unit(i, b):
                pe.wait_ge(w_ready, primed(3 * i + b + 1))
                product(nc, ps, b % 2, SEQ if COLUMNS[b] == 0 else TOK, lambda n: m.wH[:, b, n * P:(n + 1) * P], lambda n: m.wL[:, b, n * P:(n + 1) * P],
                        lambda n: m.zH[:, n, :], lambda n: m.zL[:, n, :], KD,
                        (lambda n: norm1.wait_z(pe, n)) if b == 0 else None).then_inc(qkv_done, 1)

            def scores(i, r):
                if r >= 2:
                    pe.wait_ge(s_biased, primed(ROWS * i + r - 1))
                    pe.wait_ge(ctx_copied, primed(ROWS * i + r - 1))
                rs, _ = geo[r]
                nc.tensor.matmul(ps[:, sbank(r):sbank(r) + WIN], m.qbd[:, r, :], m.kT[:, rs * GW:rs * GW + WIN], start=True, stop=True)
                nc.tensor.matmul(ps[:, sbank(r) + WIN:sbank(r) + KEYS], m.qbd[:, r, :], m.kT[:, SEQ:TOK], start=True, stop=True).then_inc(s_done, 1)

            def tail_modulation(i, q):
                pe.wait_ge(ctx_copied, primed(ROWS * i + ROWS))
                pe.wait_ge(mod_in, 16 * MPP * i + 16 * (q + 1))
                modulation_tile(nc, m, TAIL_MODS, q, 1).then_inc(mod_used, 1)

            def turn(i, r):
                pe.wait_ge(p_ready, ROWS * i + r + 1)
                pe.wait_ge(pT_ready, primed(ROWS * i + r))
                for c in range(KEYS // P):
                    ins = nc.tensor.transpose(ps[:, MISC + c * P:MISC + (c + 1) * P], S(r)[:, c * P:(c + 1) * P], m.ident[:, :])
                ins.then_inc(t_done, 1)

            def values(i, r):
                pe.wait_ge(pT_ready, primed(ROWS * i + r + 1))
                if r >= 2:
                    pe.wait_ge(o_ready, primed(ROWS * i + r - 1))
                rs, _ = geo[r]
                for c in range(KEYS // P):
                    if c >= WIN // P:
                        v = m.v0[:, SEQ // P + c - WIN // P, :]
                    else:
                        v = (m.v1 if rs % 2 else m.v0)[:, rs // 2 + c, :]
                    ins = nc.tensor.matmul(ps[:, obank(r):obank(r) + P], v, m.pT[:, r % 2, c * P:(c + 1) * P], start=(c == 0), stop=(c == KEYS // P - 1))
                ins.then_inc(o_done, 1)

            def group(i, last):
                pe.wait_ge(o_ready, primed(ROWS * i))
                pe.wait_ge(s_biased, primed(ROWS * i))
                pe.wait_ge(ctx_copied, primed(ROWS * i))
                unit(i, 0)
                pe.wait_ge(mod_copied, primed(i))
                unit(i, 1)
                pe.wait_ge(vT_ready, i + 1)
                for c in range(NV):
                    ins = nc.tensor.transpose(ps[:, MISC + c * P:MISC + (c + 1) * P], m.vT[:, c * P:(c + 1) * P], m.ident[:, :])
                ins.then_inc(v_T, 1)
                unit(i, 2)
                pe.wait_ge(v_act, 2 * i + 1)
                pe.wait_ge(v_dve, 2 * i + 1)
                pe.wait_ge(q_ready, 2 * i + 2)
                for c in range(NV - 1):
                    nc.tensor.transpose(ps[:, MISC + c * P:MISC + (c + 1) * P], m.vT[:, c * P + GW:(c + 1) * P + GW], m.ident[:, :])
                for c in range(CTX // P):
                    ins = nc.tensor.transpose(ps[:, obank(1) + c * P:obank(1) + (c + 1) * P], m.vT[:, SEQ + c * P:SEQ + (c + 1) * P], m.ident[:, :])
                ins.then_inc(v_T, 1)
                pe.wait_ge(k_act, i + 1)
                pe.wait_ge(k_dve, i + 1)
                scores(i, 0)
                scores(i, 1)
                for r in range(ROWS):
                    if r + 2 < ROWS:
                        scores(i, r + 2)
                    if r == ROWS - 2:
                        tail_modulation(i, 2)
                    if r >= 1:
                        values(i, r - 1)
                    else:
                        pe.wait_ge(v_act, 2 * i + 2)
                        pe.wait_ge(v_dve, 2 * i + 2)
                    if r in MOD_ROWS:
                        q = MOD_ROWS.index(r)
                        pe.wait_ge(mod_in, 16 * MPP * i + 16 * (q + 1))
                        modulation_tile(nc, m, MISC + KEYS, q, 1).then_inc(mod_used, 1)
                    turn(i, r)
                tail_modulation(i, 3)
                values(i, ROWS - 1)
            norm1.stats.pe(pe)
            program(pe, group)

        @block.scalar
        def _(act):
            prime(act, (pT_ready, 1), (ctx_copied, 1))

            def split(i, b):
                act.wait_ge(raw_in[b % 2], 16 * i + 16 if b == 1 else 32 * i + 16 + 8 * b)
                act.wait_ge(qkv_done, primed(3 * i))
                nc.scalar.activation(m.wH[:, b, :], m.wraw[:, b % 2, :], ACT.Copy).then_inc(w_high, 1)

            def ctx_scores(i, r):
                act.wait_ge(s_done, ROWS * i + r + 1)
                if r >= 3:
                    act.wait_ge(t_done, ROWS * i + r - 2)
                nc.scalar.activation(S(r)[:, WIN:KEYS], ps[:, sbank(r) + WIN:sbank(r) + KEYS], ACT.Copy).then_inc(ctx_copied, 1)

            def exp(i, r):
                act.wait_ge(negmax, ROWS * i + r + 1)
                nc.scalar.activation(S(r), S(r), ACT.Exp, bias=m.rowstat[:, r % 3, 0:1], accum_out=m.rowstat[:, r % 3, 1:2]).then_inc(exp_done, 1)

            def turned(i, r):
                act.wait_ge(t_done, ROWS * i + r + 1)
                if r >= 2:
                    act.wait_ge(o_done, primed(ROWS * i + r - 1))
                nc.scalar.activation(m.pT[:, r % 2, :], ps[:, MISC:MISC + KEYS], ACT.Copy).then_inc(pT_ready, 1)

            def group(i, last):
                act.wait_ge(qkv_done, primed(3 * i + 2))
                for h in range(2):
                    p0 = h * DH
                    nc.scalar.activation(m.qbd[p0:p0 + DH, :, p0:p0 + DH], ps[p0:p0 + DH, SLOT:SLOT + SEQ].rearrange("p (r c) -> p r c", c=GW),
                                         ACT.Copy, scale=DH ** -0.5).then_inc(q_ready, 1)
                act.wait_ge(v_T, 2 * i + 1)
                nc.scalar.activation(m.v0[:, 0:4, :], ps[:, MISC:MISC + BANK].rearrange("p (c f) -> p c f", f=P), ACT.Copy).then_inc(v_act, 1)
                act.wait_ge(qkv_done, primed(3 * i + 3))
                nc.scalar.activation(m.kT[:, 0:BANK], ps[:, 0:BANK], ACT.Copy).then_inc(k_act, 1)
                act.wait_ge(v_T, 2 * i + 2)
                nc.scalar.activation(m.v1[:, 0:4, :], ps[:, MISC:MISC + BANK].rearrange("p (c f) -> p c f", f=P), ACT.Copy)
                nc.scalar.activation(m.v0[:, NV:TOK // P, :], ps[:, obank(1):obank(1) + CTX].rearrange("p (c f) -> p c f", f=P), ACT.Copy).then_inc(v_act, 1)
                ctx_scores(i, 0)
                ctx_scores(i, 1)
                exp(i, 0)
                for r in range(ROWS):
                    if r >= 1:
                        turned(i, r - 1)
                    if r + 2 < ROWS:
                        ctx_scores(i, r + 2)
                    if r + 1 < ROWS:
                        exp(i, r + 1)
                    if r in (4, 6, 8) and not last:
                        split(i + 1, r // 2 - 2)
                turned(i, ROWS - 1)
            split(0, 0)
            split(0, 1)
            norm1.act(act)
            split(0, 2)
            act.wait_ge(q_zero, 1)
            program(act, group)

        @block.vector
        def _(dve):
            prime(dve, (w_ready, 1), (s_biased, 1), (o_ready, 1), (mod_copied, 1))

            def split(i, b):
                dve.wait_ge(w_high, 3 * i + b + 1)
                nc.vector.tensor_tensor(m.wL[:, b, :], m.wraw[:, b % 2, :], m.wH[:, b, :].bitcast(F32), ALU.subtract).then_inc(w_ready, 1)

            def bias_and_max(i, r):
                dve.wait_ge(s_done, ROWS * i + r + 1)
                if r >= 3:
                    dve.wait_ge(t_done, ROWS * i + r - 2)
                dr = geo[r][1]
                nc.vector.tensor_tensor(S(r)[:, 0:WIN], ps[:, sbank(r):sbank(r) + WIN],
                                        m.bias[:, dr:dr + NA_KR, :].rearrange("p r c -> p (r c)"), ALU.add).then_inc(s_biased, 1)
                dve.wait_ge(s_biased, primed(ROWS * i + r + 1))
                dve.wait_ge(ctx_copied, primed(ROWS * i + r + 1))
                nc.vector.tensor_reduce(m.rowstat[:, r % 3, 0:1], S(r), AX_X, ALU.max, negate=True).then_inc(negmax, 1)

            def normalise(i, r):
                dve.wait_ge(exp_done, ROWS * i + r + 1)
                nc.vector.reciprocal(m.rowstat[:, r % 3, 2:3], m.rowstat[:, r % 3, 1:2]).then_inc(recip, 1)
                dve.wait_ge(recip, ROWS * i + r + 1)
                nc.vector.tensor_scalar(S(r), S(r), m.rowstat[:, r % 3, 2:3], None, ALU.mult).then_inc(p_ready, 1)

            def out(i, r):
                dve.wait_ge(o_done, primed(ROWS * i + r + 1))
                for h in range(2):
                    p0 = h * DH
                    ins = nc.vector.tensor_copy(m.oT[p0:p0 + DH, r * GW:(r + 1) * GW], ps[p0:p0 + DH, obank(r) + p0:obank(r) + p0 + DH])
                ins.then_inc(o_ready, 1)

            def group(i, last):
                dve.wait_ge(qkv_done, primed(3 * i + 1))
                nc.vector.tensor_copy(m.vT[:, :], ps[:, 0:TOK]).then_inc(vT_ready, 1)
                dve.wait_ge(v_T, 2 * i + 1)
                nc.vector.tensor_copy(m.v0[:, 4:NV, :], ps[:, MISC + BANK:MISC + 2 * BANK].rearrange("p (c f) -> p c f", f=P)).then_inc(v_dve, 1)
                dve.wait_ge(qkv_done, primed(3 * i + 3))
                nc.vector.tensor_copy(m.kT[:, BANK:TOK], ps[:, BANK:TOK]).then_inc(k_dve, 1)
                dve.wait_ge(v_T, 2 * i + 2)
                nc.vector.tensor_copy(m.v1[:, 4:NV - 1, :], ps[:, MISC + BANK:MISC + BANK + 3 * P].rearrange("p (c f) -> p c f", f=P)).then_inc(v_dve, 1)
                dve.wait_ge(bias_ready, i + 1)
                dve.wait_ge(o_stored, primed(i))
                bias_and_max(i, 0)
                for r in range(ROWS):
                    if r + 1 < ROWS:
                        bias_and_max(i, r + 1)
                    normalise(i, r)
                    if r >= 2:
                        out(i, r - 2)
                    if r in (5, 7, 9) and not last:
                        split(i + 1, (r - 5) // 2)
                out(i, ROWS - 2)
                out(i, ROWS - 1)
                dve.wait_ge(mod_used, primed(MPP * i + MPP))
                half = len(MOD_ROWS)
                for g in range(2):
                    for q, n, at in ((0, half, MISC + KEYS), (half, MPP - half, TAIL_MODS)):
                        ins = nc.vector.tensor_tensor(m.mod[:, 1, g, ds(MPP * i + (MOD_FIRST + q), n)], ps[:, at + 2 * q + g:at + 2 * (q + n):2],
                                                      m.vec[:, ds(MPP * i + (VEC_AT["mod_b"] + N_MOD + MOD_FIRST + q), n)], ALU.add)
                ins.then_inc(mod_copied, 1)
            split(0, 0)
            split(0, 1)
            norm1.dve(dve)
            split(0, 2)
            program(dve, group)
            dve.wait_ge(mod_copied, primed(NP))
            for g in range(2):
                nc.vector.scalar_tensor_tensor(out=m.gain[:, 1, 1, g, :], in0=m.mod[:, 1, g, 4 * KD:5 * KD], scalar=1.0,
                                               in1=vcol(m, "norm2_g", KD, KD), op0=ALU.add, op1=ALU.mult)


def final(nc, m):
    st = Stats(nc, m, "fin", SEQ, m.diag)
    ps = m.ps
    normed, turned, low_half, high_half = [m.sem("fin_" + n) for n in ("normed", "turned", "low_half", "high_half")]
    stored = [m.sem("fin_stored0"), m.sem("fin_stored1")]

    with nc.Block() as block:
        @block.sync
        def _(sp):
            for i in range(SEQ // P):
                sp.wait_ge(low_half, i + 1)
                sp.wait_ge(high_half, i + 1)
                sp.dma_start(m.out[0, i * P:(i + 1) * P, :], m.outT[:, i % 2, :]).then_inc(stored[i % 2], 16)
            for s in range(2):
                sp.wait_ge(stored[s], 16 * (SEQ // P // 2))

        @block.scalar
        def _(act):
            st.act(act)
            for i in range(SEQ // P):
                act.wait_ge(turned, i + 1)
                if i >= 2:
                    act.wait_ge(stored[i % 2], 16 * (i // 2))
                o = (i % 2) * SLOT
                nc.scalar.activation(m.outT[:, i % 2, 0:BANK], ps[:, o:o + BANK], ACT.Copy).then_inc(low_half, 1)

        @block.tensor
        def _(pe):
            st.pe(pe)
            pe.wait_ge(normed, KD)
            for i in range(SEQ // P):
                if i >= 2:
                    pe.wait_ge(low_half, i - 1)
                    pe.wait_ge(high_half, i - 1)
                o = (i % 2) * SLOT
                for k in range(KD):
                    ins = nc.tensor.transpose(ps[:, o + k * P:o + (k + 1) * P], m.res[:, k, i * P:(i + 1) * P], m.ident[:, :])
                ins.then_inc(turned, 1)

        @block.vector
        def _(dve):
            st.dve(dve)
            for k in range(KD):
                nc.vector.scalar_tensor_tensor(out=m.res[:, k, 0:SEQ], in0=m.res[:, k, 0:SEQ], scalar=vcol(m, "final_g", k),
                                               in1=st.rstd, op0=ALU.mult, op1=ALU.mult).then_inc(normed, 1)
            for i in range(SEQ // P):
                dve.wait_ge(turned, i + 1)
                if i >= 2:
                    dve.wait_ge(stored[i % 2], 16 * (i // 2))
                o = (i % 2) * SLOT
                nc.vector.tensor_copy(m.outT[:, i % 2, BANK:D], ps[:, o + BANK:o + D]).then_inc(high_half, 1)


_INS = ['x', 'c', 'ctx', 'c_ctx', 'mod_w', 'mod_b', 'norm1_g', 'norm2_g',
        'rg_w_in', 'rg_conv_w', 'rg_conv_b', 'rg_wa', 'rg_ba', 'rg_wx', 'rg_bx', 'rg_lam', 'rg_w_out',
        'na_w_in', 'na_rpb', 'na_w_out', 'ffn_w_up', 'ffn_conv_w', 'ffn_conv_b', 'ffn_w_down', 'final_g']
_OUTS = [((1, 1024, 1024), 'float32')]


def kernel(**inputs):
    import numpy as _np
    import concourse.bacc as _bacc
    from concourse import mybir as _mybir
    from concourse.bass_utils import run_bass_kernel_spmd as _run

    nc = _bacc.Bacc("TRN2", target_bir_lowering=False, num_devices=1)
    arrays, args = {}, {}
    for name in _INS:
        a = _np.ascontiguousarray(inputs[name])
        arrays[f"in_{name}_dram"] = a
        args[name] = nc.dram_tensor(f"in_{name}_dram", a.shape, _mybir.dt.from_np(a.dtype), kind="ExternalInput").ap()
    outs = [nc.dram_tensor(f"out_{i}_dram", shape, _mybir.dt.from_np(_np.dtype(dtype)), kind="ExternalOutput").ap()
            for i, (shape, dtype) in enumerate(_OUTS)]
    build(nc, args, outs[0])
    r = _run(nc, [arrays], core_ids=[0])
    return tuple(r.results[0][f"out_{i}_dram"] for i in range(len(_OUTS)))[0]
```
